# Optimizing a Trainium2 kernel written in Bass

```python
import math
import jax, jax.numpy as jnp
from jax import lax
import numpy as np

D_MODEL = 1024
BATCH = 1
SEQ = 512
DEPTH = 1

HEAD_DIM = 128
N_HEADS = D_MODEL // HEAD_DIM
GDN_HEADS = N_HEADS // 2
NSA_HEADS = N_HEADS - GDN_HEADS
GDN_WIDTH = GDN_HEADS * HEAD_DIM
NSA_WIDTH = NSA_HEADS * HEAD_DIM
GDN_CONV = 4
GDN_CHUNK = 64
CMP_BLOCK = 32
CMP_STRIDE = 16
SEL_BLOCK = 64
N_SELECT = 16
WINDOW = 512
Q_BLOCK = 128
D_FF = 2816
FFN_CONV = 3
N_GATES = 3
IN_SPLITS = (GDN_WIDTH, GDN_WIDTH, GDN_WIDTH, GDN_WIDTH, GDN_HEADS, GDN_HEADS,
             NSA_WIDTH, HEAD_DIM, HEAD_DIM, HEAD_DIM, HEAD_DIM, HEAD_DIM, HEAD_DIM,
             N_GATES * NSA_HEADS)
N_IN = 4 * GDN_WIDTH + 2 * GDN_HEADS + NSA_WIDTH + 6 * HEAD_DIM + N_GATES * NSA_HEADS
EPS = 1e-6
NEG_INF = -1e30
FORCE_BONUS = 1e4


def rmsnorm(x, w):
    xf = x.astype(jnp.float32)
    y = xf * lax.rsqrt(jnp.mean(xf * xf, axis=-1, keepdims=True) + EPS)
    return (y * w.astype(jnp.float32)).astype(x.dtype)

def l2norm(x):
    xf = x.astype(jnp.float32)
    return xf * lax.rsqrt(jnp.sum(xf * xf, axis=-1, keepdims=True) + EPS)

def causal_dwconv(x, w, b=None):
    k = w.shape[0]
    y = lax.conv_general_dilated(x, w[:, None, :].astype(x.dtype), window_strides=(1,),
                                 padding=[(k - 1, 0)], dimension_numbers=('NWC', 'WIO', 'NWC'),
                                 feature_group_count=x.shape[-1])
    if b is not None:
        y = y + b
    return y

def masked_softmax(s, mask):
    p = jax.nn.softmax(jnp.where(mask, s, NEG_INF), axis=-1)
    return jnp.where(mask, p, 0.0)

def gated_delta_chunked(q, k, v, g, beta):
    B, S, H, dk = q.shape
    dv = v.shape[-1]
    n = S // GDN_CHUNK
    f32 = jnp.float32

    def to_chunks(t):
        t = t.astype(f32).reshape((B, n, GDN_CHUNK) + t.shape[2:])
        return jnp.moveaxis(t, 3, 1)

    q, k, v, g, beta = (to_chunks(t) for t in (q, k, v, g, beta))
    q = q * (dk ** -0.5)
    gc = jnp.cumsum(g, axis=-1)
    idx = jnp.arange(GDN_CHUNK)
    incl = idx[:, None] >= idx[None, :]
    strict = idx[:, None] > idx[None, :]
    decay = jnp.exp(jnp.where(incl, gc[..., :, None] - gc[..., None, :], NEG_INF))
    k_beta = k * beta[..., None]
    a_mat = jnp.where(strict, jnp.einsum('bhncd,bhnsd->bhncs', k_beta, k) * decay, 0.0)
    eye = jnp.eye(GDN_CHUNK, dtype=f32)
    t_mat = lax.linalg.triangular_solve(eye + a_mat, jnp.broadcast_to(eye, a_mat.shape),
                                        left_side=True, lower=True, unit_diagonal=True)
    u = t_mat @ (v * beta[..., None])
    w = t_mat @ (k_beta * jnp.exp(gc)[..., None])
    attn_intra = jnp.where(incl, jnp.einsum('bhncd,bhnsd->bhncs', q, k) * decay, 0.0)
    q_dec = q * jnp.exp(gc)[..., None]
    k_dec = k * jnp.exp(gc[..., -1:] - gc)[..., None]
    g_last = jnp.exp(gc[..., -1])

    def step(state, inp):
        u_i, w_i, qd_i, kd_i, a_i, gl_i = inp
        v_new = u_i - w_i @ state
        o_i = qd_i @ state + a_i @ v_new
        state = state * gl_i[..., None, None] + jnp.swapaxes(kd_i, -1, -2) @ v_new
        return state, o_i

    xs = tuple(jnp.moveaxis(t, 2, 0) for t in (u, w, q_dec, k_dec, attn_intra, g_last))
    state0 = jnp.zeros((B, H, dk, dv), f32)
    _, o = lax.scan(step, state0, xs)
    return jnp.transpose(o, (1, 0, 3, 2, 4)).reshape(B, S, H, dv)

def nsa_compress(kv, pos, w1, w2):
    B, S, D = kv.shape
    n_cmp = (S - CMP_BLOCK) // CMP_STRIDE + 1
    idx = jnp.arange(n_cmp)[:, None] * CMP_STRIDE + jnp.arange(CMP_BLOCK)[None, :]
    blocks = kv[:, idx] + pos
    hid = jax.nn.silu(blocks.reshape(B, n_cmp, CMP_BLOCK * D) @ w1)
    return hid @ w2

def nsa_attention(q, k_cmp, v_cmp, k_slc, v_slc, k_win, v_win, gates):
    f32 = jnp.float32
    q, k_cmp, v_cmp, k_slc, v_slc, k_win, v_win, gates = (
        t.astype(f32) for t in (q, k_cmp, v_cmp, k_slc, v_slc, k_win, v_win, gates))
    B, S, H, D = q.shape
    scale = D ** -0.5
    n_cmp = k_cmp.shape[1]
    n_sel = S // SEL_BLOCK
    n_pick = min(N_SELECT, n_sel)
    cs = jnp.arange(n_cmp) * CMP_STRIDE
    ss = jnp.arange(n_sel) * SEL_BLOCK
    ov = jnp.minimum(cs[:, None] + CMP_BLOCK, ss[None, :] + SEL_BLOCK) - jnp.maximum(cs[:, None], ss[None, :])
    overlap = jnp.clip(ov, 0, None).astype(f32) / CMP_BLOCK
    cmp_end = cs + CMP_BLOCK - 1
    k_blocks = k_slc.reshape(B, n_sel, SEL_BLOCK, D)
    v_blocks = v_slc.reshape(B, n_sel, SEL_BLOCK, D)
    k_win_pad = jnp.pad(k_win, ((0, 0), (WINDOW, 0), (0, 0)))
    v_win_pad = jnp.pad(v_win, ((0, 0), (WINDOW, 0), (0, 0)))
    blk = jnp.arange(n_sel)
    gather = jax.vmap(lambda kb, ib: kb[ib])

    def block(qi):
        t0 = qi * Q_BLOCK
        qb = lax.dynamic_slice_in_dim(q, t0, Q_BLOCK, axis=1)
        gb = lax.dynamic_slice_in_dim(gates, t0, Q_BLOCK, axis=1)
        t = t0 + jnp.arange(Q_BLOCK)
        mask_c = cmp_end[None, :] <= t[:, None]
        s_c = jnp.einsum('bqhd,bkd->bqhk', qb, k_cmp) * scale
        p_c = masked_softmax(s_c, mask_c[None, :, None, :])
        o_c = jnp.einsum('bqhk,bkd->bqhd', p_c, v_cmp)
        imp = jnp.einsum('bqhk,kj->bqj', p_c, overlap)
        cur = t // SEL_BLOCK
        valid = blk[None, :] <= cur[:, None]
        forced = (blk[None, :] == 0) | (blk[None, :] == cur[:, None]) | (blk[None, :] == cur[:, None] - 1)
        imp = jnp.where(valid[None], imp + jnp.where(forced, FORCE_BONUS, 0.0)[None], NEG_INF)
        _, sel = lax.top_k(imp, n_pick)
        ks = gather(k_blocks, sel).reshape(B, Q_BLOCK, n_pick * SEL_BLOCK, D)
        vs = gather(v_blocks, sel).reshape(B, Q_BLOCK, n_pick * SEL_BLOCK, D)
        pos_s = (sel[..., None] * SEL_BLOCK + jnp.arange(SEL_BLOCK)).reshape(B, Q_BLOCK, n_pick * SEL_BLOCK)
        mask_s = pos_s <= t[None, :, None]
        s_s = jnp.einsum('bqhd,bqkd->bqhk', qb, ks) * scale
        p_s = masked_softmax(s_s, mask_s[:, :, None, :])
        o_s = jnp.einsum('bqhk,bqkd->bqhd', p_s, vs)
        kw = lax.dynamic_slice_in_dim(k_win_pad, t0, Q_BLOCK + WINDOW, axis=1)
        vw = lax.dynamic_slice_in_dim(v_win_pad, t0, Q_BLOCK + WINDOW, axis=1)
        pos_w = t0 - WINDOW + jnp.arange(Q_BLOCK + WINDOW)
        mask_w = (pos_w[None, :] <= t[:, None]) & (pos_w[None, :] > t[:, None] - WINDOW) & (pos_w[None, :] >= 0)
        s_w = jnp.einsum('bqhd,bkd->bqhk', qb, kw) * scale
        p_w = masked_softmax(s_w, mask_w[None, :, None, :])
        o_w = jnp.einsum('bqhk,bkd->bqhd', p_w, vw)
        return gb[..., 0:1] * o_c + gb[..., 1:2] * o_s + gb[..., 2:3] * o_w

    out = lax.map(block, jnp.arange(S // Q_BLOCK))
    return jnp.moveaxis(out, 0, 1).reshape(B, S, H, D)

def hybrid_layer(x, c, ada_w, ada_b, norm1_w, w_in, gdn_conv_w, gdn_A_log, gdn_dt_bias,
                 gdn_out_norm_w, nsa_q_norm_w, nsa_k_norm_cmp, nsa_k_norm_slc, nsa_k_norm_win,
                 cmp_k_pos, cmp_k_w1, cmp_k_w2, cmp_v_pos, cmp_v_w1, cmp_v_w2, w_out,
                 norm2_w, ffn_w_up, ffn_conv_w, ffn_conv_b, ffn_w_down):
    f32 = jnp.float32
    B, S, _ = x.shape
    mod = jax.nn.silu(c) @ ada_w + ada_b
    shift1, scale1, gate1, shift2, scale2, gate2 = jnp.split(mod[:, None, :], 6, axis=-1)

    h = rmsnorm(x, norm1_w) * (1 + scale1) + shift1
    proj = h @ w_in
    offsets = np.cumsum(IN_SPLITS)[:-1].tolist()
    (gq, gk, gv, gz, ga, gbeta, nq, kc, vc, ksl, vsl, kwn, vwn, ng) = jnp.split(proj, offsets, axis=-1)

    qkv = jax.nn.silu(causal_dwconv(jnp.concatenate([gq, gk, gv], axis=-1), gdn_conv_w))
    gq, gk, gv = jnp.split(qkv, 3, axis=-1)
    hd = (B, S, GDN_HEADS, HEAD_DIM)
    q_g = l2norm(gq.reshape(hd))
    k_g = l2norm(gk.reshape(hd))
    v_g = gv.reshape(hd)
    beta = jax.nn.sigmoid(gbeta.astype(f32))
    log_decay = -jnp.exp(gdn_A_log.astype(f32)) * jax.nn.softplus(ga.astype(f32) + gdn_dt_bias.astype(f32))
    o_g = gated_delta_chunked(q_g, k_g, v_g, log_decay, beta)
    o_g = rmsnorm(o_g, gdn_out_norm_w) * jax.nn.silu(gz.reshape(hd).astype(f32))

    q_n = rmsnorm(nq.reshape(B, S, NSA_HEADS, HEAD_DIM), nsa_q_norm_w)
    k_cmp = rmsnorm(nsa_compress(kc, cmp_k_pos, cmp_k_w1, cmp_k_w2), nsa_k_norm_cmp)
    v_cmp = nsa_compress(vc, cmp_v_pos, cmp_v_w1, cmp_v_w2)
    k_slc = rmsnorm(ksl, nsa_k_norm_slc)
    k_win = rmsnorm(kwn, nsa_k_norm_win)
    gates = jax.nn.sigmoid(ng.reshape(B, S, NSA_HEADS, N_GATES))
    o_n = nsa_attention(q_n, k_cmp, v_cmp, k_slc, vsl, k_win, vwn, gates)

    mixed = jnp.concatenate([o_g.reshape(B, S, GDN_WIDTH), o_n.reshape(B, S, NSA_WIDTH)], axis=-1)
    x = x + gate1 * (mixed.astype(x.dtype) @ w_out)

    h2 = rmsnorm(x, norm2_w) * (1 + scale2) + shift2
    up = causal_dwconv(h2 @ ffn_w_up, ffn_conv_w, ffn_conv_b)
    a, b = jnp.split(up, 2, axis=-1)
    x = x + gate2 * ((jax.nn.silu(a) * b) @ ffn_w_down)
    return x

def first_inputs(seed: int = 0) -> dict:
    key = jax.random.key(seed)
    ks = jax.random.split(key, 32)
    f32 = jnp.float32
    L = DEPTH

    def nrm(k, shape, s):
        return jax.random.normal(k, shape, f32) * s

    def gain(k, n):
        return 1.0 + 0.02 * jax.random.normal(k, (L, n), f32)

    dt = jnp.exp(jax.random.uniform(ks[8], (L, GDN_HEADS), f32, math.log(1e-3), math.log(1e-1)))
    return {
        'x': nrm(ks[0], (BATCH, SEQ, D_MODEL), 1.0),
        'c': nrm(ks[1], (BATCH, D_MODEL), 1.0),
        'ada_w': nrm(ks[2], (L, D_MODEL, 6 * D_MODEL), 0.5 * D_MODEL ** -0.5),
        'ada_b': nrm(ks[3], (L, 6 * D_MODEL), 0.02),
        'norm1_w': gain(ks[4], D_MODEL),
        'w_in': nrm(ks[5], (L, D_MODEL, N_IN), D_MODEL ** -0.5),
        'gdn_conv_w': nrm(ks[6], (L, GDN_CONV, 3 * GDN_WIDTH), GDN_CONV ** -0.5),
        'gdn_A_log': jnp.log(jax.random.uniform(ks[7], (L, GDN_HEADS), f32, 1.0, 16.0)),
        'gdn_dt_bias': dt + jnp.log(-jnp.expm1(-dt)),
        'gdn_out_norm_w': gain(ks[9], HEAD_DIM),
        'nsa_q_norm_w': gain(ks[10], HEAD_DIM),
        'nsa_k_norm_cmp': gain(ks[11], HEAD_DIM),
        'nsa_k_norm_slc': gain(ks[12], HEAD_DIM),
        'nsa_k_norm_win': gain(ks[13], HEAD_DIM),
        'cmp_k_pos': nrm(ks[14], (L, CMP_BLOCK, HEAD_DIM), 0.02),
        'cmp_k_w1': nrm(ks[15], (L, CMP_BLOCK * HEAD_DIM, HEAD_DIM), (CMP_BLOCK * HEAD_DIM) ** -0.5),
        'cmp_k_w2': nrm(ks[16], (L, HEAD_DIM, HEAD_DIM), HEAD_DIM ** -0.5),
        'cmp_v_pos': nrm(ks[17], (L, CMP_BLOCK, HEAD_DIM), 0.02),
        'cmp_v_w1': nrm(ks[18], (L, CMP_BLOCK * HEAD_DIM, HEAD_DIM), (CMP_BLOCK * HEAD_DIM) ** -0.5),
        'cmp_v_w2': nrm(ks[19], (L, HEAD_DIM, HEAD_DIM), HEAD_DIM ** -0.5),
        'w_out': nrm(ks[20], (L, D_MODEL, D_MODEL), D_MODEL ** -0.5),
        'norm2_w': gain(ks[21], D_MODEL),
        'ffn_w_up': nrm(ks[22], (L, D_MODEL, 2 * D_FF), D_MODEL ** -0.5),
        'ffn_conv_w': nrm(ks[23], (L, FFN_CONV, 2 * D_FF), FFN_CONV ** -0.5),
        'ffn_conv_b': nrm(ks[24], (L, 2 * D_FF), 0.02),
        'ffn_w_down': nrm(ks[25], (L, D_FF, D_MODEL), D_FF ** -0.5),
    }

def first_block(x, c, ada_w, ada_b, norm1_w, w_in, gdn_conv_w, gdn_A_log, gdn_dt_bias,
              gdn_out_norm_w, nsa_q_norm_w, nsa_k_norm_cmp, nsa_k_norm_slc, nsa_k_norm_win,
              cmp_k_pos, cmp_k_w1, cmp_k_w2, cmp_v_pos, cmp_v_w1, cmp_v_w2, w_out,
              norm2_w, ffn_w_up, ffn_conv_w, ffn_conv_b, ffn_w_down):
    for l in range(DEPTH):
        x = hybrid_layer(x, c, ada_w[l], ada_b[l], norm1_w[l], w_in[l], gdn_conv_w[l], gdn_A_log[l],
                         gdn_dt_bias[l], gdn_out_norm_w[l], nsa_q_norm_w[l], nsa_k_norm_cmp[l],
                         nsa_k_norm_slc[l], nsa_k_norm_win[l], cmp_k_pos[l], cmp_k_w1[l], cmp_k_w2[l],
                         cmp_v_pos[l], cmp_v_w1[l], cmp_v_w2[l], w_out[l], norm2_w[l], ffn_w_up[l],
                         ffn_conv_w[l], ffn_conv_b[l], ffn_w_down[l])
    return x


POOL_WIDTH = D_MODEL // 2
POOL_GROUPS = 4
POOL_GROUP_WIDTH = POOL_WIDTH // POOL_GROUPS
POOL_WINDOWS = (2, 4, 8, 16)
CONV_WIDTH = D_MODEL // 2
CONV_KERNEL = 31
N_BRANCHES = 2
IN_WIDTH = POOL_WIDTH + 2 * CONV_WIDTH + N_BRANCHES * D_MODEL
PEER_HEADS = 8
PEER_KEY_DIM = 256
PEER_HALF_DIM = PEER_KEY_DIM // 2
N_KEYS = 128
N_EXPERTS = N_KEYS * N_KEYS
PEER_TOPK_HALF = 16
PEER_TOPK = 16
PEER_CHUNK = 128
N_MOD = 6


def rmsnorm_2(x, g):
    xf = x.astype(jnp.float32)
    y = xf * lax.rsqrt(jnp.mean(xf * xf, axis=-1, keepdims=True) + EPS)
    return (y * g.astype(jnp.float32)).astype(x.dtype)

def layernorm(x, g, b):
    xf = x.astype(jnp.float32)
    mu = jnp.mean(xf, axis=-1, keepdims=True)
    var = jnp.mean(jnp.square(xf - mu), axis=-1, keepdims=True)
    y = (xf - mu) * lax.rsqrt(var + EPS)
    return (y * g.astype(jnp.float32) + b.astype(jnp.float32)).astype(x.dtype)

def causal_window_mean(xg, w):
    s = xg.shape[1]
    xf = xg.astype(jnp.float32)
    cs = jnp.cumsum(xf, axis=1)
    shifted = jnp.pad(cs, ((0, 0), (w, 0), (0, 0)))[:, :s]
    count = jnp.minimum(jnp.arange(1, s + 1), w).astype(jnp.float32)[None, :, None]
    return ((cs - shifted) / count).astype(xg.dtype)

def pool_branch(p, pool_w, pool_scale, pool_up):
    b, s, _ = p.shape
    pooled = jnp.concatenate(
        [causal_window_mean(p[..., i * POOL_GROUP_WIDTH:(i + 1) * POOL_GROUP_WIDTH], w)
         for i, w in enumerate(POOL_WINDOWS)], axis=-1)
    mixed = (pooled - p).reshape(b, s, POOL_GROUPS, POOL_GROUP_WIDTH)
    mixed = jnp.einsum('bsgc,gcd->bsgd', mixed, pool_w).reshape(b, s, POOL_WIDTH)
    return (mixed * pool_scale) @ pool_up

def conformer_branch(a, dw_kernel, dw_bias, ln_g, ln_b, conv_out):
    glu = a[..., :CONV_WIDTH] * jax.nn.sigmoid(a[..., CONV_WIDTH:])
    y = lax.conv_general_dilated(
        glu, dw_kernel[:, None, :].astype(glu.dtype), window_strides=(1,),
        padding=[(CONV_KERNEL - 1, 0)], dimension_numbers=('NWC', 'WIO', 'NWC'),
        feature_group_count=CONV_WIDTH) + dw_bias
    y = layernorm(y, ln_g, ln_b)
    y = y * jax.nn.sigmoid(y)
    return y @ conv_out

def peer(h, w_query, keys_1, keys_2, expert_u, expert_v):
    b, s, d = h.shape
    flat = h.reshape(b * s // PEER_CHUNK, PEER_CHUNK, d)

    def chunk_fn(hc):
        q = (hc @ w_query).reshape(PEER_CHUNK, PEER_HEADS, PEER_KEY_DIM)
        s1 = jnp.einsum('chk,nk->chn', q[..., :PEER_HALF_DIM], keys_1)
        s2 = jnp.einsum('chk,nk->chn', q[..., PEER_HALF_DIM:], keys_2)
        v1, i1 = lax.top_k(s1, PEER_TOPK_HALF)
        v2, i2 = lax.top_k(s2, PEER_TOPK_HALF)
        cand = (v1[..., :, None] + v2[..., None, :]).reshape(PEER_CHUNK, PEER_HEADS, -1)
        cand_idx = (i1[..., :, None] * N_KEYS + i2[..., None, :]).reshape(PEER_CHUNK, PEER_HEADS, -1)
        top_s, pos = lax.top_k(cand, PEER_TOPK)
        experts = jnp.take_along_axis(cand_idx, pos, axis=-1)
        gate = jax.nn.softmax(top_s.astype(jnp.float32), axis=-1).astype(hc.dtype)
        u = jnp.take(expert_u, experts, axis=0)
        act = jax.nn.gelu(jnp.einsum('chkd,cd->chk', u, hc))
        v = jnp.take(expert_v, experts, axis=0)
        return jnp.einsum('chk,chkd->cd', gate * act, v)

    return lax.map(chunk_fn, flat).reshape(b, s, d)

def second_inputs(seed: int = 0) -> dict:
    key = jax.random.key(seed)
    ks = jax.random.split(key, 24)

    def nrm(k, shape, scale):
        return jax.random.normal(k, shape, jnp.float32) * scale

    def gain(k, shape):
        return 1.0 + 0.05 * jax.random.normal(k, shape, jnp.float32)

    L = DEPTH
    return {
        "x": nrm(ks[0], (BATCH, SEQ, D_MODEL), 1.0),
        "c": nrm(ks[1], (BATCH, D_MODEL), 1.0),
        "ada_w": nrm(ks[2], (L, D_MODEL, N_MOD * D_MODEL), 0.5 * D_MODEL ** -0.5),
        "ada_b": nrm(ks[3], (L, N_MOD * D_MODEL), 0.01),
        "norm1_g": gain(ks[4], (L, D_MODEL)),
        "w_in": nrm(ks[5], (L, D_MODEL, IN_WIDTH), D_MODEL ** -0.5),
        "b_in": nrm(ks[6], (L, IN_WIDTH), 0.01),
        "pool_w": nrm(ks[7], (L, POOL_GROUPS, POOL_GROUP_WIDTH, POOL_GROUP_WIDTH), POOL_GROUP_WIDTH ** -0.5),
        "pool_scale": gain(ks[8], (L, POOL_WIDTH)),
        "pool_up": nrm(ks[9], (L, POOL_WIDTH, D_MODEL), POOL_WIDTH ** -0.5),
        "dw_kernel": nrm(ks[10], (L, CONV_KERNEL, CONV_WIDTH), CONV_KERNEL ** -0.5),
        "dw_bias": nrm(ks[11], (L, CONV_WIDTH), 0.01),
        "conv_ln_g": gain(ks[12], (L, CONV_WIDTH)),
        "conv_ln_b": nrm(ks[13], (L, CONV_WIDTH), 0.01),
        "conv_out": nrm(ks[14], (L, CONV_WIDTH, D_MODEL), CONV_WIDTH ** -0.5),
        "w_out": nrm(ks[15], (L, D_MODEL, D_MODEL), D_MODEL ** -0.5),
        "norm2_g": gain(ks[16], (L, D_MODEL)),
        "w_query": nrm(ks[17], (L, D_MODEL, PEER_HEADS * PEER_KEY_DIM), D_MODEL ** -0.5),
        "sub_keys_1": nrm(ks[18], (L, N_KEYS, PEER_HALF_DIM), PEER_HALF_DIM ** -0.5),
        "sub_keys_2": nrm(ks[19], (L, N_KEYS, PEER_HALF_DIM), PEER_HALF_DIM ** -0.5),
        "expert_u": nrm(ks[20], (L, N_EXPERTS, D_MODEL), D_MODEL ** -0.5),
        "expert_v": nrm(ks[21], (L, N_EXPERTS, D_MODEL), PEER_HEADS ** -0.5),
        "final_g": gain(ks[22], (D_MODEL,)),
    }

def second_block(x, c, ada_w, ada_b, norm1_g, w_in, b_in, pool_w, pool_scale, pool_up,
              dw_kernel, dw_bias, conv_ln_g, conv_ln_b, conv_out, w_out, norm2_g,
              w_query, sub_keys_1, sub_keys_2, expert_u, expert_v, final_g):
    c_act = jax.nn.silu(c)
    for l in range(DEPTH):
        mod = c_act @ ada_w[l] + ada_b[l]
        shift1, scale1, gate1, shift2, scale2, gate2 = [
            m[:, None, :] for m in jnp.split(mod, N_MOD, axis=-1)]

        h = rmsnorm_2(x, norm1_g[l]) * (1.0 + scale1) + shift1
        proj = h @ w_in[l] + b_in[l]
        p = proj[..., :POOL_WIDTH]
        a = proj[..., POOL_WIDTH:POOL_WIDTH + 2 * CONV_WIDTH]
        g = proj[..., POOL_WIDTH + 2 * CONV_WIDTH:]
        y_pool = pool_branch(p, pool_w[l], pool_scale[l], pool_up[l])
        y_conv = conformer_branch(a, dw_kernel[l], dw_bias[l], conv_ln_g[l], conv_ln_b[l], conv_out[l])
        merged = jax.nn.sigmoid(g[..., :D_MODEL]) * y_pool + jax.nn.sigmoid(g[..., D_MODEL:]) * y_conv
        x = x + gate1 * (merged @ w_out[l])

        h2 = rmsnorm_2(x, norm2_g[l]) * (1.0 + scale2) + shift2
        x = x + gate2 * peer(h2, w_query[l], sub_keys_1[l], sub_keys_2[l], expert_u[l], expert_v[l])
    return rmsnorm_2(x, final_g)


def setup_inputs(seed=0):
    out = dict(first_inputs(seed))
    for name, value in second_inputs(seed + 1).items():
        if name != "x":
            out[name + "_2"] = value
    return out


def reference(
    x, c, ada_w, ada_b, norm1_w, w_in, gdn_conv_w, gdn_A_log, gdn_dt_bias, gdn_out_norm_w,
    nsa_q_norm_w, nsa_k_norm_cmp, nsa_k_norm_slc, nsa_k_norm_win, cmp_k_pos, cmp_k_w1, cmp_k_w2,
    cmp_v_pos, cmp_v_w1, cmp_v_w2, w_out, norm2_w, ffn_w_up, ffn_conv_w, ffn_conv_b, ffn_w_down,
    c_2, ada_w_2, ada_b_2, norm1_g_2, w_in_2, b_in_2, pool_w_2, pool_scale_2, pool_up_2,
    dw_kernel_2, dw_bias_2, conv_ln_g_2, conv_ln_b_2, conv_out_2, w_out_2, norm2_g_2, w_query_2,
    sub_keys_1_2, sub_keys_2_2, expert_u_2, expert_v_2, final_g_2,
):
    x = first_block(
        x, c, ada_w, ada_b, norm1_w, w_in, gdn_conv_w, gdn_A_log, gdn_dt_bias, gdn_out_norm_w,
        nsa_q_norm_w, nsa_k_norm_cmp, nsa_k_norm_slc, nsa_k_norm_win, cmp_k_pos, cmp_k_w1,
        cmp_k_w2, cmp_v_pos, cmp_v_w1, cmp_v_w2, w_out, norm2_w, ffn_w_up, ffn_conv_w,
        ffn_conv_b, ffn_w_down,
    )
    return second_block(
        x, c_2, ada_w_2, ada_b_2, norm1_g_2, w_in_2, b_in_2, pool_w_2, pool_scale_2, pool_up_2,
        dw_kernel_2, dw_bias_2, conv_ln_g_2, conv_ln_b_2, conv_out_2, w_out_2, norm2_g_2,
        w_query_2, sub_keys_1_2, sub_keys_2_2, expert_u_2, expert_v_2, final_g_2,
    )


_drawn_inputs = setup_inputs


def setup_inputs(seed=0):
    import zlib

    import numpy as np

    out = dict(_drawn_inputs(seed))
    spreads = {}
    factors = {'norm1_w': 8.0,
     'gdn_out_norm_w': 8.0,
     'nsa_q_norm_w': 8.0,
     'nsa_k_norm_cmp': 45.268,
     'nsa_k_norm_slc': 21.926,
     'nsa_k_norm_win': 8.0,
     'cmp_k_pos': 45.818,
     'cmp_k_w1': 2.761,
     'cmp_k_w2': 2.863,
     'cmp_v_pos': 64.0,
     'norm2_w': 7.225,
     'ffn_conv_b': 7.922,
     'ada_b_2': 5.859,
     'norm1_g_2': 5.164,
     'b_in_2': 64.0,
     'pool_scale_2': 20.548,
     'dw_bias_2': 64.0,
     'conv_ln_g_2': 58.104,
     'conv_ln_b_2': 200.0,
     'norm2_g_2': 32.64}
    for name, (base, spread) in spreads.items():
        noise = np.random.default_rng([zlib.crc32(name.encode()), seed]).standard_normal(out[name].shape)
        drawn = base * np.exp(spread * noise) if base else spread * noise
        out[name] = __import__('jax').numpy.asarray(drawn.astype(out[name].dtype))
    for name, factor in factors.items():
        out[name] = (out[name] * factor).astype(out[name].dtype)
    return out
```

```python
import numpy as np
import concourse.bass as bass
from concourse import mybir
from contextlib import ExitStack

F32 = mybir.dt.float32
U32 = mybir.dt.uint32
ALU = mybir.AluOpType
ACT = mybir.ActivationFunctionType
X = mybir.AxisListType.X

P = 128
S = 512
D = 1024
KT = D // P
NC = S // P
NH = 4
HD = 128
SCALE = HD ** -0.5
EPS = 1e-6
NEG = -1e30
NCMP = (S - 32) // 16 + 1
CMP_L, CMP_STRIDE = 32, 16
FF = 2816
FT = FF // P
SLOTS = 4
WIDE = FF // 2
LEVELS = 7
NROW = 2 * HD + 2 * NH + 3 * NH
TAPS = 31
PW = (2, 4, 8, 16)
HEADS, TOPK, NKEYS = 8, 16, 128
RING = 8
BATCH = 4

def _cols(widths):
    out, at = {}, 0
    for name, w in widths:
        out[name] = (at, at + w)
        at += w
    return out, at

CONST, NCONST = _cols([
    ("ident", P), ("ones", P), ("upper", P), ("strict", P), ("causal", P), ("levels", LEVELS * P),
    ("cmpneg", NC * NCMP), ("cmpmask", NC * NCMP), ("poolcnt", 4 * 16), ("iota", 16), ("eps", 1), ("one", 1)])
PARAM, NPARAM = _cols([
    ("c", KT), ("c_2", KT), ("ada_b", 48), ("ada_b_2", 48), ("norm1", KT), ("norm2", KT), ("norm1_2", KT),
    ("norm2_2", KT), ("final", KT), ("gconv", 12 * 4), ("a_log", 16), ("dt", 16), ("onorm", 1), ("qnorm", 1),
    ("kn_cmp", 1), ("kn_slc", 1), ("kn_win", 1), ("pos_k", CMP_L), ("pos_v", CMP_L), ("fconv", 2 * FT * 3),
    ("fbias", 2 * FT), ("b_in", 28), ("pscale", 4), ("dw", 4 * TAPS), ("dwb", 4), ("lng", 4), ("lnb", 4)])
MATS, NMATS = _cols([("w2k", P), ("w2v", P), ("keys1", P), ("keys2", P), ("poolw", 4 * P)])
STREAM = [("ada", 48, D), ("ada_2", 48, D), ("w_in", 24, D), ("cmp", 8, D), ("w_out", 8, D), ("up", 2 * FT, D),
          ("down", 16, WIDE), ("w_in_2", 28, D), ("branch", 8, D), ("w_out_2", 8, D), ("query", 16, D)]
FIRST = {}
_at = 0
for _n, _b, _w in STREAM:
    FIRST[_n] = _at
    _at += _b


class Count:

    def __init__(self):
        self.n, self.off, self.per = {}, {}, []

    def __call__(self, sem):
        k = id(sem)
        self.n[k] = self.n.get(k, 0) + 1
        return self.n[k] + self.off.get(k, 0)

    def enter(self, i, *per):
        self.per = [(id(s), v) for s, v in per]
        self.at = dict(self.n)
        self.off = {k: i * v for k, v in self.per}

    def leave(self, passes):
        per = dict(self.per)
        for k, v in self.n.items():
            got = v - self.at.get(k, 0)
            assert got == per.get(k, 0), got
            self.n[k] = self.at.get(k, 0) + got * passes
        self.off, self.per = {}, []


def build(nc, a, out):
    ctx = ExitStack()
    with ctx:
        def sb(name, shape, dt=F32):
            return ctx.enter_context(nc.sbuf_tensor(name, shape, dt))

        xT = sb("xT", [P, KT, S])
        hT = sb("hT", [P, KT, S])
        ring = sb("ring", [P, SLOTS, WIDE])
        const = sb("const", [P, NCONST])
        param = sb("param", [P, NPARAM])
        mats = sb("mats", [P, NMATS])
        sq = sb("sq", [P, 2, S])
        rs = sb("rs", [P, 2, S])
        mod = sb("mod", [P, 2, 48])
        eff = sb("eff", [P, 4, KT])
        silc = sb("silc", [P, 2, KT])
        AR = 32320
        arena = sb("arena", [P, AR])

        def area(at, *dims):
            n = int(np.prod(dims))
            assert at + n <= AR, (at, n)
            v = arena[:, at:at + n]
            names = "abcd"[:len(dims)]
            if len(dims) == 1:
                return v
            return v.rearrange("p (" + " ".join(names) + ") -> p " + " ".join(names),
                               **dict(zip(names[1:], dims[1:])))

        def cst(name):
            return const[:, CONST[name][0]:CONST[name][1]]

        def par(name, i=0, n=1):
            b = PARAM[name][0] + i
            return param[:, b:b + n]

        def mat(name):
            return mats[:, MATS[name][0]:MATS[name][1]]

        ident, ones, eps, one = cst("ident"), cst("ones"), cst("eps"), cst("one")

        modrow = arena[0:1, 0:2 * S].rearrange("p (u n) -> p u n", u=2)
        qkv = area(0, 12, S)
        mix = area(6144, 8, S)
        kcvc = area(10240, 2, S)
        kswn = area(11264, 2, S)
        vrow = area(12288, NC, 2, HD)
        roww = area(13312, KT, NROW)
        cv = area(15520, 2, S)
        small = area(16544, NC, 20)
        sgm = area(16624, NC, 16)
        gsm = area(16688, 8, 16)
        g3 = area(16816, 3, 16)
        e3 = area(16864, 3, 16)
        kb = area(16912, 16)
        gcl = area(16928, 2, 16)
        Tm = area(2048, NH, NC, P)
        TT = area(0, NH, NC, P)
        Am = area(4096, NH, NC, P)
        Y = area(13312, NH, NC, P)
        t1 = area(16960, 2, S)
        t2 = area(17984, 2, S)
        kbg = area(19008, NH, NC, P)
        kd = area(21056, NH, NC, P)
        vb = area(23104, NH, NC, P)
        attnT = area(25152, NH, NC, P)
        At = area(27200, NH, NC, P)
        qdT = area(29248, NH, S)
        Ug = area(19008, NH, NC, P)
        Ib = area(13312, NH, NC, P)
        eg = area(31296, S)
        Sst = area(31296, NH, HD)
        vn = area(31808, NH, HD)
        Um = Tm
        wT = Am
        oT = area(13312, NH, S)
        kcp = area(0, 2, CMP_L, NCMP)
        hid = area(19008, 2, NCMP)
        kct = area(19072, NCMP)
        vcr = area(19104, HD)
        Pm = area(19232, 2, 2, S)
        Pc = area(21280, 2, 32)
        sc = area(21344, 2, 32)
        PT = area(21408, 2, 9, P)
        mx = area(23712, 2, 16)
        gT = area(0, FT, S)
        y0 = area(FT * S, 2, S)
        y1 = area(FT * S + 1024, 2, S)
        sa = area(FT * S + 2048, 2, S)
        sgT = area(0, 16, S)
        pT = area(8192, 4, 16 + S)
        glu = area(10304, 4, 30 + S)
        a1 = area(12472, 2, S)
        a2 = area(13496, 2, S)
        cs1 = area(14520, 16 + S)
        cs2 = area(15048, 16 + S)
        mx4 = area(15576, 4, S)
        pmT = area(17624, 4, S)
        yc = area(19672, 4, S)
        m1 = area(21720, 2, S)
        mg = area(22744, 8, S)
        lnm = area(26840, S)
        lnd = area(27352, 2, S)
        qT = area(0, 16, S)
        hrow = area(8192, NC, D)
        sS = area(12288, 16, NKEYS)
        s2 = area(14336, 2, 256)
        vals = area(14848, 16, 16)
        idf = area(15104, 16, 16)
        cand = area(15360, HEADS, 256)
        eqv = area(17408, HEADS, 16, 16)
        tops = area(19456, HEADS, 16)
        gate = area(19584, NC, HEADS, 16)
        ifl = area(20096, 4, HEADS * 16)
        sm = area(20608, 4, 16)
        ring_e = area(0, RING, 2 * D)
        prow = area(21120, D)
        junk = area(22144, D)
        dots = area(23168, 4, BATCH)
        diag = area(23232, 2, BATCH, P)
        hrow2 = area(24256, NC, D)
        hrow = hrow2
        ecur = sb("ecur", [P, 2, RING], U32)
        idx = sb("idx", [P, 16, 16], U32)
        pos = sb("pos", [P, 3, HEADS * 16], U32)
        expi = sb("expi", [P, NC * HEADS + 1, 16], U32)

        PS = ctx.enter_context(nc.psum_tensor("PS", [P, 8, S], F32))

        def sem(name):
            return ctx.enter_context(nc.semaphore(name))

        act_step = sem("act_step")
        am_ready = sem("am_ready")
        att_ready = sem("att_ready")
        av_done = sem("av_done")
        b_in = sem("b_in")
        blocks_done = sem("blocks_done")
        conv_ready = sem("conv_ready")
        dec_exp = sem("dec_exp")
        dec_in = sem("dec_in")
        diag_ready = sem("diag_ready")
        dots_ready = sem("dots_ready")
        e3_in = sem("e3_in")
        e3_ready = sem("e3_ready")
        ecur_ready = sem("ecur_ready")
        eg_ready = sem("eg_ready")
        ff_ready = sem("ff_ready")
        fy_ready = sem("fy_ready")
        g_ready = sem("g_ready")
        gate_e = sem("gate_e")
        gate_ea = sem("gate_ea")
        gate_ln = sem("gate_ln")
        gate_nz = sem("gate_nz")
        gate_sg = sem("gate_sg")
        gc_done = sem("gc_done")
        gelu_ready = sem("gelu_ready")
        glu_ready = sem("glu_ready")
        h_ready = sem("h_ready")
        hid_ready = sem("hid_ready")
        hr_done = sem("hr_done")
        hr_ready = sem("hr_ready")
        hs_normed = sem("hs_normed")
        hs_ready = sem("hs_ready")
        hs_std = sem("hs_std")
        hs_used = sem("hs_used")
        inputs_loaded = sem("inputs_loaded")
        kc_done = sem("kc_done")
        kc_ready = sem("kc_ready")
        kcp_ready = sem("kcp_ready")
        kv_done = sem("kv_done")
        ln_in = sem("ln_in")
        ln_mu = sem("ln_mu")
        ln_sq = sem("ln_sq")
        ln_std = sem("ln_std")
        ln_sum1 = sem("ln_sum1")
        ln_sum2 = sem("ln_sum2")
        ln_y = sem("ln_y")
        m_half = sem("m_half")
        merged = sem("merged")
        mod_ready = sem("mod_ready")
        modcol_done = sem("modcol_done")
        modrow_ready = sem("modrow_ready")
        negm_ready = sem("negm_ready")
        normed = sem("normed")
        o_done = sem("o_done")
        o_ready = sem("o_ready")
        og_ready = sem("og_ready")
        out_done = sem("out_done")
        p_ready = sem("p_ready")
        params_loaded = sem("params_loaded")
        pm_ready = sem("pm_ready")
        pn_ready = sem("pn_ready")
        pool_done = sem("pool_done")
        pool_seen = sem("pool_seen")
        pq_done = sem("pq_done")
        prep_done = sem("prep_done")
        prep_ps = sem("prep_ps")
        prow_ready = sem("prow_ready")
        pscaled = sem("pscaled")
        pt2_done = sem("pt2_done")
        pt_act = sem("pt_act")
        pt_done = sem("pt_done")
        pt_vec = sem("pt_vec")
        q_ready = sem("q_ready")
        qkv_ready = sem("qkv_ready")
        routed = sem("routed")
        row_evac = sem("row_evac")
        rows_done = sem("rows_done")
        rows_used = sem("rows_used")
        s_done = sem("s_done")
        sa_ready = sem("sa_ready")
        sc2_done = sem("sc2_done")
        sc2_ready = sem("sc2_ready")
        sc_done = sem("sc_done")
        sg_ready = sem("sg_ready")
        silu_c_ready = sem("silu_c_ready")
        sm_exp = sem("sm_exp")
        sm_in = sem("sm_in")
        sq_ready = sem("sq_ready")
        sq_used = sem("sq_used")
        state_ready = sem("state_ready")
        std_ready = sem("std_ready")
        tr_ready = sem("tr_ready")
        tt_ready = sem("tt_ready")
        u_ready = sem("u_ready")
        ug_ready = sem("ug_ready")
        uw_done = sem("uw_done")
        vc_ready = sem("vc_ready")
        vec_step = sem("vec_step")
        vnew_ready = sem("vnew_ready")
        w_ready = sem("w_ready")
        w_ready2 = sem("w_ready2")
        ws_done = sem("ws_done")
        x1_ready = sem("x1_ready")
        x2_ready = sem("x2_ready")
        x3_ready = sem("x3_ready")
        x4_ready = sem("x4_ready")
        y_done = sem("y_done")
        y_ready = sem("y_ready")
        yc_ready = sem("yc_ready")
        zq_ready = sem("zq_ready")
        slot_ready = [sem(f"slot{j}_ready") for j in range(SLOTS)]
        bank_free = [sem(f"bank{j}_free") for j in range(4)]
        row_landed = [sem(f"expert_row{j}_ready") for j in range(RING)]

        block = ctx.enter_context(nc.Block())

        @block.sync
        def _(sp):
            sp.dma_start(param[:], a["param"]).then_inc(params_loaded, 16)
            first = STREAM[0]
            for j in range(SLOTS):
                sp.dma_start(ring[:, j, :D], a["ada"][j]).then_inc(slot_ready[j], 16)
            sp.dma_start(const[:], a["const"]).then_inc(inputs_loaded, 16)
            sp.dma_start(xT[:], a["x"]).then_inc(inputs_loaded, 16)
            sp.dma_start(roww, a["roww"]).then_inc(inputs_loaded, 16)
            sp.dma_start(mats[:], a["mats"]).then_inc(inputs_loaded, 16)
            for name, blocks, width in STREAM:
                lo = 1 if name == first[0] else 0
                with sp.Fori(lo, blocks // SLOTS) as i:
                    for j in range(SLOTS):
                        sp.wait_ge(blocks_done, FIRST[name] + i * SLOTS + j - SLOTS + 1)
                        sp.dma_start(ring[:, j, :width],
                                     a[name][bass.ds(i * SLOTS + j, 1)].rearrange("o p n -> p (o n)")
                                     ).then_inc(slot_ready[j], 16)
            sp.wait_ge(h_ready, 5 * KT)
            sp.dma_start(out, hT[:]).then_inc(out_done, 16)
            sp.wait_ge(out_done, 16)


        @block.tensor
        def _(pe):
            def mm(o, l, r, start=True, stop=True):
                return nc.tensor.matmul(o, l, r, start=start, stop=stop)

            def tiles(j, n=KT):
                return [ring[:, j, k * P:(k + 1) * P] for k in range(n)]

            def gemm(name, rhs, freed, base, first=0, last=None):
                last = dict((n, b) for n, b, _ in STREAM)[name] if last is None else last
                with pe.Fori(first // SLOTS, last // SLOTS) as i:
                    for j in range(SLOTS):
                        pe.wait_ge(slot_ready[j], 16 * (FIRST[name] // SLOTS) + 16 + i * 16)
                        pe.wait_ge(freed, base + i * SLOTS + j - 3)
                        for k, w in enumerate(tiles(j)):
                            ins = mm(PS[:, j, :], w, rhs[:, k, :], k == 0, k == KT - 1)
                        ins.then_inc(blocks_done, 1)

            pe.wait_ge(inputs_loaded, 64)
            for blk, name in ((0, "ada"), (1, "ada_2")):
                pe.wait_ge(silu_c_ready, blk + 1)

                def group(g, par):
                    for j in range(SLOTS):
                        pe.wait_ge(slot_ready[j], 16 * (FIRST[name] // SLOTS) + 16 + g * 16)
                        for u in range(2):
                            k = 2 * j + u
                            ins = mm(PS[0:1, 4 + par, :], silc[:, blk, k:k + 1], ring[:, j, u * S:(u + 1) * S],
                                     k == 0, k == KT - 1)
                        ins.then_inc(blocks_done, 1)

                def turn(g, par):
                    pe.wait_ge(modrow_ready, 12 * blk + g + 1)
                    for q in range(4):
                        ins = mm(PS[:, 6 + blk, bass.ds(g * 4 + q, 1)] if not isinstance(g, int) else
                                 PS[:, 6 + blk, g * 4 + q:g * 4 + q + 1],
                                 modrow[0:1, par, q * P:(q + 1) * P], one[0:1, :])
                    ins.then_inc(modcol_done, 1)

                group(0, 0)
                with pe.Fori(0, 5) as i:
                    group(i * 2 + 1, 1)
                    turn(i * 2, 0)
                    group(i * 2 + 2, 0)
                    turn(i * 2 + 1, 1)
                group(11, 1)
                turn(10, 0)
                turn(11, 1)

            def norm(n):
                for k in range(KT):
                    pe.wait_ge(sq_ready, KT * n + k + 1)
                    mm(PS[:, 7, :], ones, sq[:, k % 2, :], k == 0, k == KT - 1).then_inc(sq_used, 1)

            pe.wait_ge(mod_ready, 2)
            norm(0)
            pe.wait_ge(h_ready, KT)
            for c in range(NC):
                for k in range(KT):
                    ins = mm(PS[:, c, :NROW], hT[:, k, c * P:(c + 1) * P], roww[:, k, :], k == 0, k == KT - 1)
                ins.then_inc(rows_done, 1)
            pe.wait_ge(row_evac, 2 * NC)
            gemm("w_in", hT, row_evac, 2 * NC, 0, 4)
            gemm("w_in", hT, conv_ready, 0, 4, 16)
            gemm("w_in", hT, zq_ready, -12, 16, 24)
            pe.wait_ge(g_ready, 1)
            mm(PS[:, 4, 0:16], cst("upper"), gsm[:, 5, :])
            mm(PS[:, 4, 16:32], ones, gsm[:, 5, :]).then_inc(gc_done, 1)
            pe.wait_ge(e3_in, 1)

            def head_norm(n, width=S):
                pe.wait_ge(hs_ready, n + 1)
                if n >= 4:
                    pe.wait_ge(hs_std, n - 3)
                mm(PS[:, 4 + n % 4, :width], ones, sq[:, n % 2, :width]).then_inc(hs_used, 1)

            for n in range(14):
                head_norm(n)
            pe.wait_ge(hs_normed, 14)
            pe.wait_ge(ug_ready, 2)
            for h in range(NH):
                b = 4 * (h % 2)
                if h >= 2:
                    pe.wait_ge(prep_done, h - 1)
                    pe.wait_ge(eg_ready, h - 1)
                mm(PS[:, b, :], ones, Ug[:, h, :, :].rearrange("p c n -> p (c n)"))
                mm(PS[:, b + 1, :], ones, Ib[:, h, :, :].rearrange("p c n -> p (c n)"))
                for c in range(NC):
                    t = slice(c * P, (c + 1) * P)
                    mm(PS[:, b + 2, t], qkv[:, 4 + h, t], qkv[:, 4 + h, t])
                for c in range(NC):
                    t = slice(c * P, (c + 1) * P)
                    ins = mm(PS[:, b + 3, t], qkv[:, 4 + h, t], qkv[:, h, t])
                ins.then_inc(prep_ps, 1)
            pe.wait_ge(prep_done, NH)
            for n in range(8):
                if n >= 2:
                    pe.wait_ge(kv_done, n - 1)
                for c in range(NC):
                    t = slice(c * P, (c + 1) * P)
                    ins = nc.tensor.transpose(PS[:, n % 2, t], qkv[:, 4 + n, t], ident)
                ins.then_inc(tr_ready, 1)
            pe.wait_ge(kv_done, 8)
            def second(i, h):
                pe.wait_ge(y_ready, i * NH + h + 1)
                pe.wait_ge(tt_ready, i * NH + h + 3)
                for c in range(NC):
                    mm(PS[:, 2 + h % 2, c * P:(c + 1) * P], TT[:, h, c, :], Y[:, h, c, :])
                for c in range(NC):
                    ins = mm(PS[:, 4 + h % 2, c * P:(c + 1) * P], Y[:, h, c, :], TT[:, h, c, :])
                ins.then_inc(pq_done, 1)

            with pe.Fori(0, LEVELS) as i:
                for h in range(NH):
                    pe.wait_ge(am_ready, i * NH + h + 1)
                    pe.wait_ge(tt_ready, i * NH + h + 1)
                    for c in range(NC):
                        ins = mm(PS[:, h % 2, c * P:(c + 1) * P], Am[:, h, c, :], Tm[:, h, c, :])
                    ins.then_inc(y_done, 1)
                    if h:
                        second(i, h - 1)
                second(i, NH - 1)
            pe.wait_ge(tt_ready, NH * LEVELS + NH)
            for h in range(NH):
                b = 2 * (h % 2)
                if h >= 2:
                    pe.wait_ge(u_ready, h - 1)
                    pe.wait_ge(w_ready, h - 1)
                for c in range(NC):
                    mm(PS[:, b, c * P:(c + 1) * P], TT[:, h, c, :], vb[:, h, c, :])
                for c in range(NC):
                    ins = mm(PS[:, b + 1, c * P:(c + 1) * P], kbg[:, h, c, :], TT[:, h, c, :])
                ins.then_inc(uw_done, 1)
            pe.wait_ge(u_ready, NH)
            pe.wait_ge(w_ready, NH)
            for c in range(NC):
                t = slice(c * P, (c + 1) * P)
                pe.wait_ge(state_ready, NH * c + 1)
                for h in range(NH):
                    hh = slice(h * P, (h + 1) * P)
                    ins = mm(PS[:, 0, hh], wT[:, h, c, :], Sst[:, h, :])
                ins.then_inc(ws_done, 1)
                pe.wait_ge(vnew_ready, c + 1)
                if c >= 2:
                    pe.wait_ge(o_ready, c - 1)
                for h in range(NH):
                    hh = slice(h * P, (h + 1) * P)
                    mm(PS[:, 1 + c % 2, hh], Sst[:, h, :], qdT[:, h, t], True, False)
                    ins = mm(PS[:, 1 + c % 2, hh], vn[:, h, :], attnT[:, h, c, :], False, True)
                ins.then_inc(o_done, 1)
                for h in range(NH):
                    ins = mm(PS[:, 3, h * P:(h + 1) * P], kd[:, h, c, :], vn[:, h, :])
                ins.then_inc(s_done, 1)
            for h in range(NH):
                head_norm(14 + h)
            pe.wait_ge(og_ready, NH)
            pe.wait_ge(kcp_ready, 2)
            for z in range(2):
                for b in range(4):
                    j = b
                    pe.wait_ge(slot_ready[j], 16 * (FIRST["cmp"] // SLOTS + z + 1))
                    for k in range(KT):
                        n = b * KT + k
                        ins = mm(PS[:, z, :NCMP], ring[:, j, k * P:(k + 1) * P], kcp[:, z, n, :], n == 0, n == CMP_L - 1)
                    ins.then_inc(blocks_done, 1)
            pe.wait_ge(hid_ready, 2)
            mm(PS[:, 2, :NCMP], mat("w2k"), hid[:, 0, :])
            mm(PS[:NCMP, 3, :HD], hid[:, 1, :], mat("w2v")).then_inc(kc_done, 1)
            head_norm(18, NCMP)
            pe.wait_ge(hs_normed, 19)
            pe.wait_ge(vc_ready, 1)
            def scores(n):
                c, h = divmod(n, NH)
                if n >= 2:
                    pe.wait_ge(p_ready, 3 * (n - 1))
                    pe.wait_ge(att_ready, n - 1)
                q = mix[:, 4 + h, c * P:(c + 1) * P]
                N = (c + 1) * P
                mm(PS[:, 2 * (n % 2), :N], q, kswn[:, 0, :N])
                mm(PS[:, 2 * (n % 2) + 1, :N], q, kswn[:, 1, :N])
                mm(PS[:, 4 + n % 2, :NCMP], q, kct[:, :NCMP]).then_inc(sc_done, 1)

            scores(0)
            for n in range(NC * NH):
                c, h = divmod(n, NH)
                if n + 1 < NC * NH:
                    scores(n + 1)
                pe.wait_ge(pn_ready, 3 * (n + 1))
                if n >= 1:
                    pe.wait_ge(pt_act, 2 * n)
                    pe.wait_ge(pt_vec, n)
                for k in range(c + 1):
                    nc.tensor.transpose(PS[:, 6, k * P:(k + 1) * P], Pm[:, n % 2, 0, k * P:(k + 1) * P], ident)
                for k in range(c + 1):
                    nc.tensor.transpose(PS[:, 7, k * P:(k + 1) * P], Pm[:, n % 2, 1, k * P:(k + 1) * P], ident)
                nc.tensor.transpose(PS[:NCMP, 4 + n % 2, P:2 * P], Pc[:, n % 2, :NCMP], ident
                                    ).then_inc(pt_done, 1)
                pe.wait_ge(pt_act, 2 * (n + 1))
                pe.wait_ge(pt_vec, n + 1)
                o = PS[:, 4 + n % 2, 2 * P:3 * P]
                for k in range(c + 1):
                    for z in range(2):
                        mm(o, vrow[:, k, z, :], PT[:, n % 2, 4 * z + k, :], k + z == 0, False)
                mm(o, vcr[:NCMP, :], PT[:NCMP, n % 2, 8, :], False, True).then_inc(av_done, 1)
            pe.wait_ge(att_ready, NC * NH)
            gemm("w_out", mix, att_ready, NC * NH, 0, 4)
            gemm("w_out", mix, x1_ready, 0, 4, 8)
            norm(1)
            pe.wait_ge(h_ready, 2 * KT)
            pe.wait_ge(x1_ready, 8)
            gemm("up", hT, x1_ready, 8, 0, 4)
            gemm("up", hT, fy_ready, 0, 4)
            pe.wait_ge(ff_ready, FT)
            for m in range(KT):
                if m >= 4:
                    pe.wait_ge(x2_ready, m - 3)
                for u in range(2):
                    q = 2 * m + u
                    pe.wait_ge(slot_ready[q % SLOTS], 16 * ((FIRST["down"] + q) // SLOTS + 1))
                    for k in range(FT // 2):
                        kk = u * (FT // 2) + k
                        ins = mm(PS[:, m % 4, :], ring[:, q % SLOTS, k * P:(k + 1) * P], gT[:, kk, :], kk == 0, kk == FT - 1)
                    ins.then_inc(blocks_done, 1)
            norm(2)
            pe.wait_ge(h_ready, 3 * KT)
            gemm("w_in_2", hT, x2_ready, 8, 0, 4)
            gemm("w_in_2", hT, sg_ready, 0, 4)
            for g in range(4):
                pe.wait_ge(pm_ready, g + 1)
                pe.wait_ge(sg_ready, 28)
                mm(PS[:, g, :], mat("poolw")[:, g * P:(g + 1) * P], mx4[:, g, :]).then_inc(pool_done, 1)
            pe.wait_ge(ln_in, 1)
            for g in range(4):
                ins = mm(PS[:, 4, :], ones, yc[:, g, :], g == 0, g == 3)
            ins.then_inc(ln_sum1, 1)
            for g in range(4):
                pe.wait_ge(ln_sq, g + 1)
                mm(PS[:, 5, :], ones, sq[:, g % 2, :], g == 0, g == 3).then_inc(ln_sum2, 1)
            pe.wait_ge(yc_ready, 4)
            pe.wait_ge(pscaled, 4)
            for m in range(KT):
                j, b = m % SLOTS, 2 * (m % 2)
                pe.wait_ge(slot_ready[j], 16 * ((FIRST["branch"] + m) // SLOTS + 1))
                if m >= 2:
                    pe.wait_ge(m_half, m - 1)
                for k in range(4):
                    mm(PS[:, b, :], ring[:, j, k * P:(k + 1) * P], pmT[:, k, :], k == 0, k == 3)
                for k in range(4):
                    ins = mm(PS[:, b + 1, :], ring[:, j, (4 + k) * P:(5 + k) * P], yc[:, k, :], k == 0, k == 3)
                ins.then_inc(blocks_done, 1)
            pe.wait_ge(merged, 8)
            gemm("w_out_2", mg, merged, 8, 0, 4)
            gemm("w_out_2", mg, x3_ready, 0, 4)
            norm(3)
            pe.wait_ge(h_ready, 4 * KT)
            pe.wait_ge(x3_ready, 8)
            gemm("query", hT, x3_ready, 8, 0, 4)
            gemm("query", hT, q_ready, 0, 4)
            for n in range(2 * NC):
                c, half = divmod(n, 2)
                if n >= 2:
                    pe.wait_ge(hr_ready, n - 1)
                for k in range(4):
                    ins = nc.tensor.transpose(PS[:, 4 + n % 2, k * P:(k + 1) * P],
                                              hT[:, 4 * half + k, c * P:(c + 1) * P], ident)
                ins.then_inc(hr_done, 1)
            pe.wait_ge(q_ready, 16)
            for c in range(NC):
                for g in range(4):
                    if c:
                        pe.wait_ge(sc2_ready, 4 * (c - 1) + g + 1)
                    for u in range(4):
                        m = 4 * g + u
                        ins = mm(PS[:, g, u * P:(u + 1) * P], qT[:, m, c * P:(c + 1) * P],
                                 mat("keys1") if m % 2 == 0 else mat("keys2"))
                    ins.then_inc(sc2_done, 1)
            def head(c, h, start=False, stop=False):
                for u in range(4):
                    pe.wait_ge(diag_ready, (c * HEADS) * 4 + h * 4 + u + 1)
                    for k in range(BATCH):
                        r = (u * BATCH + k) % RING
                        for v in range(2):
                            ins = mm(PS[:, 4 * (c % 2) + v, :], diag[:, u % 2, k, :],
                                     ring_e[:, r, D + v * S:D + (v + 1) * S],
                                     start and u + k == 0, stop and u == 3 and k == BATCH - 1)
                    ins.then_inc(rows_used, 1)

            for c in range(NC):
                head(c, 0, start=True)
                with pe.Fori(1, HEADS - 1) as h:
                    head(c, h)
                head(c, HEADS - 1, stop=True)
                pe.wait_ge(prow_ready, 2 * (c + 1))
                for v in range(2):
                    if c:
                        pe.wait_ge(x4_ready, KT * c)
                    for k in range(4):
                        ins = nc.tensor.transpose(PS[:, 2 + v, k * P:(k + 1) * P], prow[:, (4 * v + k) * P:(4 * v + k + 1) * P], ident)
                    ins.then_inc(pt2_done, 1)
            norm(4)

        @block.scalar
        def _(act):
            n = Count()
            A = nc.scalar.activation

            act.wait_ge(params_loaded, 16)
            A(silc[:, 0, :], par("c", 0, KT), ACT.Silu).then_inc(silu_c_ready, 1)
            act.wait_ge(silu_c_ready, n(silu_c_ready))
            A(silc[:, 1, :], par("c_2", 0, KT), ACT.Silu).then_inc(silu_c_ready, 1)
            act.wait_ge(silu_c_ready, n(silu_c_ready))
            for blk, name in ((0, "ada"), (1, "ada_2")):
                def row(g, par_):
                    act.wait_ge(blocks_done, FIRST[name] + SLOTS + g * SLOTS)
                    A(modrow[0:1, par_, :], PS[0:1, 4 + par_, :], ACT.Copy).then_inc(modrow_ready, 1)

                if blk:
                    act.wait_ge(modcol_done, 11)
                row(0, 0)
                if blk:
                    act.wait_ge(modcol_done, 12)
                row(1, 1)
                with act.Fori(1, 6) as i:
                    n.enter(i - 1, (modrow_ready, 2))
                    for u in range(2):
                        act.wait_ge(modcol_done, 12 * blk + u - 1 + i * 2)
                        row(i * 2 + u, u)
                    n.leave(5)

            def norm(z, col, shift, final=None, base=0):
                for k in range(KT):
                    if KT * z + k >= 2:
                        act.wait_ge(sq_used, KT * z + k - 1)
                    if final is not None:
                        act.wait_ge(final, base + k + 1)
                    A(sq[:, k % 2, :], xT[:, k, :], ACT.Square).then_inc(sq_ready, 1)
                    act.wait_ge(sq_ready, n(sq_ready))
                act.wait_ge(sq_used, KT * (z + 1))
                A(rs[:, 0, :], PS[:, 7, :], ACT.Sqrt, bias=eps, scale=1.0 / D).then_inc(std_ready, 1)
                act.wait_ge(std_ready, n(std_ready))
                for k in range(KT):
                    act.wait_ge(normed, KT * z + k + 1)
                    if shift is None:
                        A(hT[:, k, :], hT[:, k, :], ACT.Copy, scale=par("final", k)).then_inc(h_ready, 1)
                        act.wait_ge(h_ready, n(h_ready))
                    else:
                        A(hT[:, k, :], hT[:, k, :], ACT.Identity, bias=shift(k), scale=eff[:, col, k:k + 1]).then_inc(h_ready, 1)
                        act.wait_ge(h_ready, n(h_ready))

            act.wait_ge(inputs_loaded, 64)
            act.wait_ge(mod_ready, 2)
            norm(0, 0, lambda k: mod[:, 0, k:k + 1])
            for c in range(NC):
                act.wait_ge(rows_done, c + 1)
                A(vrow[:, c, :, :].rearrange("p z d -> p (z d)"), PS[:, c, :2 * HD], ACT.Copy).then_inc(row_evac, 1)
                act.wait_ge(row_evac, n(row_evac))
                A(small[:, c, :], PS[:, c, 2 * HD:NROW], ACT.Copy).then_inc(row_evac, 1)
                act.wait_ge(row_evac, n(row_evac))
            with act.Fori(0, 6) as i:
                n.enter(i, (qkv_ready, 2))
                for u in range(2):
                    act.wait_ge(conv_ready, i * 2 + u + 1)
                    A(qkv[:, bass.ds(i * 2 + u, 1), :].rearrange("p o n -> p (o n)"), cv[:, u, :], ACT.Silu).then_inc(qkv_ready, 1)
                    act.wait_ge(qkv_ready, n(qkv_ready))
                n.leave(6)
            for m in range(12, 24):
                act.wait_ge(blocks_done, FIRST["w_in"] + m + 1)
                dst = mix[:, m - 12, :] if m < 20 else (kcvc[:, m - 20, :] if m < 22 else kswn[:, m - 22, :])
                A(dst, PS[:, m % 4, :], ACT.Silu if m < 16 else ACT.Copy).then_inc(zq_ready, 1)
                act.wait_ge(zq_ready, n(zq_ready))
            A(sgm, small[:, :, NH:], ACT.Sigmoid).then_inc(gate_sg, 1)
            act.wait_ge(gate_sg, n(gate_sg))
            act.wait_ge(gate_nz, 1)
            A(gsm[:, 2, :], gsm[:, 1, :], ACT.Exp).then_inc(gate_e, 1)
            act.wait_ge(gate_e, n(gate_e))
            A(gsm[:, 3, :], gsm[:, 2, :], ACT.Ln, bias=one).then_inc(gate_ln, 1)
            act.wait_ge(gate_ln, n(gate_ln))
            A(gsm[:, 4, :], par("a_log", 0, 16), ACT.Exp).then_inc(gate_ea, 1)
            act.wait_ge(gate_ea, n(gate_ea))
            act.wait_ge(e3_in, 1)
            A(e3, g3, ACT.Exp).then_inc(e3_ready, 1)
            act.wait_ge(e3_ready, n(e3_ready))

            def head_norm(t, src, scale, width=S):
                if t >= 2:
                    act.wait_ge(hs_used, t - 1)
                A(sq[:, t % 2, :width], src, ACT.Square).then_inc(hs_ready, 1)
                act.wait_ge(hs_ready, n(hs_ready))
                act.wait_ge(hs_used, t + 1)
                if t >= 2:
                    act.wait_ge(hs_normed, t - 1)
                A(rs[:, t % 2, :width], PS[:, 4 + t % 4, :width], ACT.Sqrt, bias=eps, scale=scale).then_inc(hs_std, 1)
                act.wait_ge(hs_std, n(hs_std))

            for t in range(14):
                src = qkv[:, t, :] if t < 8 else (mix[:, t - 4, :] if t < 12 else kswn[:, t - 12, :])
                head_norm(t, src, 1.0 if t < 8 else 1.0 / HD)
            for h in range(NH):
                act.wait_ge(prep_ps, h + 1)
                act.wait_ge(dec_in, h + 1)
                A(eg, PS[:, 4 * (h % 2), :], ACT.Exp).then_inc(eg_ready, 1)
                act.wait_ge(eg_ready, n(eg_ready))
                A(t1[:, h % 2, :], t1[:, h % 2, :], ACT.Exp).then_inc(dec_exp, 1)
                act.wait_ge(dec_exp, n(dec_exp))
            with act.Fori(0, LEVELS) as i:
                n.enter(i, (y_ready, NH))
                for h in range(NH):
                    act.wait_ge(y_done, i * NH + h + 1)
                    A(Y[:, h, :, :].rearrange("p c n -> p (c n)"), PS[:, h % 2, :], ACT.Copy).then_inc(y_ready, 1)
                    act.wait_ge(y_ready, n(y_ready))
                n.leave(LEVELS)
            for h in range(NH):
                act.wait_ge(uw_done, h + 1)
                A(Um[:, h, :, :].rearrange("p c n -> p (c n)"), PS[:, 2 * (h % 2), :], ACT.Copy).then_inc(u_ready, 1)
                act.wait_ge(u_ready, n(u_ready))
            for c in range(NC):
                act.wait_ge(o_done, c + 1)
                A(oT[:, :, c * P:(c + 1) * P], PS[:, 1 + c % 2, :].rearrange("p (h n) -> p h n", h=NH), ACT.Copy).then_inc(o_ready, 1)
                act.wait_ge(o_ready, n(o_ready))
            for h in range(NH):
                head_norm(14 + h, oT[:, h, :], 1.0 / HD)
            for z in range(2):
                act.wait_ge(blocks_done, FIRST["cmp"] + 4 * (z + 1))
                A(hid[:, z, :], PS[:, z, :NCMP], ACT.Silu).then_inc(hid_ready, 1)
                act.wait_ge(hid_ready, n(hid_ready))
            act.wait_ge(kc_done, 1)
            A(kct[:, :NCMP], PS[:, 2, :NCMP], ACT.Copy).then_inc(kc_ready, 1)
            act.wait_ge(kc_ready, n(kc_ready))
            A(vcr[:NCMP, :], PS[:NCMP, 3, :HD], ACT.Copy).then_inc(vc_ready, 1)
            act.wait_ge(vc_ready, n(vc_ready))
            head_norm(18, kct[:, :NCMP], 1.0 / HD, NCMP)
            def exps(t):
                c, h = divmod(t, NH)
                N = (c + 1) * P
                act.wait_ge(negm_ready, t + 1)
                m = mx[:, t % 2, :]
                A(Pc[:, t % 2, :NCMP], sc[:, t % 2, :NCMP], ACT.Exp, scale=SCALE, accum_out=m[:, 6:7]).then_inc(p_ready, 1)
                act.wait_ge(p_ready, n(p_ready))
                A(Pm[:, t % 2, 0, :N], PS[:, 2 * (t % 2), :N], ACT.Exp, bias=m[:, 4:5], scale=SCALE, accum_out=m[:, 7:8]).then_inc(p_ready, 1)
                act.wait_ge(p_ready, n(p_ready))
                A(Pm[:, t % 2, 1, :N], PS[:, 2 * (t % 2) + 1, :N], ACT.Exp, bias=m[:, 5:6], scale=SCALE, accum_out=m[:, 8:9]).then_inc(p_ready, 1)
                act.wait_ge(p_ready, n(p_ready))

            exps(0)
            for t in range(NC * NH):
                c, h = divmod(t, NH)
                N = (c + 1) * P
                if t + 1 < NC * NH:
                    exps(t + 1)
                act.wait_ge(pt_done, t + 1)
                A(PT[:, t % 2, 0:c + 1, :], PS[:, 6, :N].rearrange("p (k q) -> p k q", q=P), ACT.Copy).then_inc(pt_act, 1)
                act.wait_ge(pt_act, n(pt_act))
                A(PT[:NCMP, t % 2, 8, :], PS[:NCMP, 4 + t % 2, P:2 * P], ACT.Copy).then_inc(pt_act, 1)
                act.wait_ge(pt_act, n(pt_act))
                act.wait_ge(av_done, t + 1)
                A(mix[:, 4 + h, c * P:(c + 1) * P], PS[:, 4 + t % 2, 2 * P:3 * P], ACT.Copy).then_inc(att_ready, 1)
                act.wait_ge(att_ready, n(att_ready))
            norm(1, 1, lambda k: mod[:, 0, 24 + k:25 + k], x1_ready, 0)
            with act.Fori(0, FT // 2) as i:
                n.enter(i, (sa_ready, 2))
                for u in range(2):
                    act.wait_ge(fy_ready, i * 4 + 2 * u + 1)
                    A(sa[:, u, :], y0[:, u, :], ACT.Silu).then_inc(sa_ready, 1)
                    act.wait_ge(sa_ready, n(sa_ready))
                n.leave(FT // 2)
            norm(2, 2, lambda k: mod[:, 1, k:k + 1], x2_ready, 0)
            for m in range(28):
                act.wait_ge(blocks_done, FIRST["w_in_2"] + m + 1)
                src = PS[:, m % 4, :]
                b = par("b_in", m)
                if m < 4:
                    A(pT[:, m, 16:], src, ACT.Identity, bias=b).then_inc(sg_ready, 1)
                    act.wait_ge(sg_ready, n(sg_ready))
                elif m < 12:
                    t = (m - 4) // 2
                    if m % 2 == 0 and t >= 2:
                        act.wait_ge(glu_ready, t - 1)
                    if m % 2 == 0:
                        A(a1[:, t % 2, :], src, ACT.Identity, bias=b).then_inc(sg_ready, 1)
                        act.wait_ge(sg_ready, n(sg_ready))
                    else:
                        A(a2[:, t % 2, :], src, ACT.Sigmoid, bias=b).then_inc(sg_ready, 1)
                        act.wait_ge(sg_ready, n(sg_ready))
                else:
                    A(sgT[:, m - 12, :], src, ACT.Sigmoid, bias=b).then_inc(sg_ready, 1)
                    act.wait_ge(sg_ready, n(sg_ready))
            for g in range(4):
                act.wait_ge(pool_done, g + 1)
                A(pmT[:, g, :], PS[:, g, :], ACT.Copy, scale=par("pscale", g)).then_inc(pscaled, 1)
                act.wait_ge(pscaled, n(pscaled))
            act.wait_ge(ln_sum1, 1)
            A(lnm, PS[:, 4, :], ACT.Copy, scale=1.0 / S).then_inc(ln_mu, 1)
            act.wait_ge(ln_mu, n(ln_mu))
            for g in range(4):
                act.wait_ge(ln_y, g + 1)
                if g >= 2:
                    act.wait_ge(ln_sum2, g - 1)
                A(sq[:, g % 2, :], yc[:, g, :], ACT.Square).then_inc(ln_sq, 1)
                act.wait_ge(ln_sq, n(ln_sq))
            act.wait_ge(ln_sum2, 4)
            A(rs[:, 0, :], PS[:, 5, :], ACT.Sqrt, bias=eps, scale=1.0 / S).then_inc(ln_std, 1)
            act.wait_ge(ln_std, n(ln_std))
            for g in range(4):
                act.wait_ge(ln_y, 4 + g + 1)
                A(yc[:, g, :], yc[:, g, :], ACT.Silu).then_inc(yc_ready, 1)
                act.wait_ge(yc_ready, n(yc_ready))
            norm(3, 3, lambda k: mod[:, 1, 24 + k:25 + k], x3_ready, 0)
            for m in range(16):
                act.wait_ge(blocks_done, FIRST["query"] + m + 1)
                A(qT[:, m, :], PS[:, m % 4, :], ACT.Copy).then_inc(q_ready, 1)
                act.wait_ge(q_ready, n(q_ready))
            for c in range(NC):
                for g in range(4):
                    act.wait_ge(sc2_done, 4 * c + g + 1)
                    if c:
                        act.wait_ge(routed, c)
                    A(sS[:, 4 * g:4 * g + 4, :], PS[:, g, :].rearrange("p (u n) -> p u n", u=4), ACT.Copy).then_inc(sc2_ready, 1)
                    act.wait_ge(sc2_ready, n(sc2_ready))
                act.wait_ge(sm_in, c + 1)
                A(gate[:, c, :, :], gate[:, c, :, :], ACT.Exp).then_inc(sm_exp, 1)
                act.wait_ge(sm_exp, n(sm_exp))
            for c in range(NC):
                with act.Fori(0, HEADS) as h:
                    n.enter(h, (gelu_ready, 4), (w_ready2, 4 * BATCH), (diag_ready, 4), (act_step, 4 * (BATCH - 1)))
                    for u in range(4):
                        act.wait_ge(dots_ready, c * HEADS * 16 + h * 16 + BATCH * (u + 1))
                        A(dots[:, 2 + u % 2, :], dots[:, u % 2, :], ACT.Gelu_apprx_tanh).then_inc(gelu_ready, 1)
                        act.wait_ge(gelu_ready, n(gelu_ready))
                        for k in range(BATCH):
                            A(dots[:, 2 + u % 2, k:k + 1], dots[:, 2 + u % 2, k:k + 1], ACT.Copy,
                                  scale=gate[:, c, bass.ds(h, 1), u * BATCH + k]).then_inc(w_ready2, 1)
                            act.wait_ge(w_ready2, n(w_ready2))
                        for k in range(BATCH):
                            A(diag[:, u % 2, k, :], ident, ACT.Copy, scale=dots[:, 2 + u % 2, k:k + 1]).then_inc(diag_ready if k == BATCH - 1 else act_step, 1)
                            act.wait_ge(diag_ready if k == BATCH - 1 else act_step, n(diag_ready if k == BATCH - 1 else act_step))
                    n.leave(HEADS)
                act.wait_ge(rows_used, 4 * HEADS * (c + 1))
                if c:
                    act.wait_ge(pt2_done, 2 * c)
                for v in range(2):
                    A(prow[:, v * S:(v + 1) * S], PS[:, 4 * (c % 2) + v, :], ACT.Copy).then_inc(prow_ready, 1)
                    act.wait_ge(prow_ready, n(prow_ready))
            norm(4, None, None, x4_ready, KT * (NC - 1))

        @block.vector
        def _(dve):
            n = Count()
            V = nc.vector

            def tt(o, x, y, op):
                return V.tensor_tensor(out=o, in0=x, in1=y, op=op)

            def ts(o, x, s1, s2, op0, op1):
                return V.tensor_scalar(o, x, s1, s2, op0, op1)

            def stt(o, x, s_, y, op0, op1):
                return V.scalar_tensor_tensor(out=o, in0=x, scalar=s_, in1=y, op0=op0, op1=op1)

            def copy(o, x):
                return V.tensor_copy(o, x)

            def last(v, many):
                return v.unsqueeze(len(v.shape)).to_broadcast(list(v.shape) + [many])

            def mid(v, *many):
                for q in many:
                    v = v.unsqueeze(1)
                return v.to_broadcast([v.shape[0], *many, v.shape[-1]])

            def flat(v):
                return v.rearrange("p c n -> p (c n)")


            MUL, ADD, SUB, MAX, MIN = ALU.mult, ALU.add, ALU.subtract, ALU.max, ALU.min
            dve.wait_ge(params_loaded, 16)
            for blk in range(2):
                dve.wait_ge(modcol_done, 12 * (blk + 1))
                tt(mod[:, blk, :], PS[:, 6 + blk, 0:48], par("ada_b" if blk == 0 else "ada_b_2", 0, 48), ADD).then_inc(vec_step, 1)
                dve.wait_ge(vec_step, n(vec_step))
                for u, g in enumerate(("norm1", "norm2") if blk == 0 else ("norm1_2", "norm2_2")):
                    stt(eff[:, 2 * blk + u, :], mod[:, blk, 8 + 24 * u:16 + 24 * u], 1.0, par(g, 0, KT), ADD, MUL).then_inc(mod_ready if u else vec_step, 1)
                    dve.wait_ge(mod_ready if u else vec_step, n(mod_ready if u else vec_step))

            def norm(t):
                dve.wait_ge(std_ready, t + 1)
                V.reciprocal(rs[:, 0, :], rs[:, 0, :]).then_inc(vec_step, 1)
                dve.wait_ge(vec_step, n(vec_step))
                for k in range(KT):
                    tt(hT[:, k, :], xT[:, k, :], rs[:, 0, :], MUL).then_inc(normed, 1)
                    dve.wait_ge(normed, n(normed))

            dve.wait_ge(inputs_loaded, 64)
            norm(0)
            def conv4(i, fresh):
                for j in range(SLOTS):
                    dve.wait_ge(blocks_done, FIRST["w_in"] + i * SLOTS + j + 1)
                    if not fresh or j >= 2:
                        dve.wait_ge(qkv_ready, i * SLOTS + j - 1)

                    def tap(t):
                        return param[:, bass.ds(i * 16 + (PARAM["gconv"][0] + 4 * j + t), 1)]
                    o = cv[:, j % 2, :]
                    ts(o, PS[:, j, :], tap(3), None, MUL, ALU.bypass).then_inc(vec_step, 1)
                    dve.wait_ge(vec_step, n(vec_step))
                    for t in (1, 2, 3):
                        stt(o[:, t:], PS[:, j, :S - t], tap(3 - t), o[:, t:], MUL, ADD).then_inc(conv_ready if t == 3 else vec_step, 1)
                        dve.wait_ge(conv_ready if t == 3 else vec_step, n(conv_ready if t == 3 else vec_step))

            conv4(0, True)
            with dve.Fori(1, 3) as i:
                n.enter(i - 1, (conv_ready, SLOTS), (vec_step, 3 * SLOTS))
                conv4(i, False)
                n.leave(2)
            dve.wait_ge(zq_ready, 12)
            dve.wait_ge(qkv_ready, 12)
            dve.wait_ge(row_evac, 2 * NC)
            tt(gsm[:, 0, :].rearrange("p (c h) -> p c h", h=NH), small[:, :, 0:NH], par("dt", 0, 16).rearrange("p (c h) -> p c h", h=NH), ADD).then_inc(vec_step, 1)
            dve.wait_ge(vec_step, n(vec_step))
            stt(gsm[:, 1, :], gsm[:, 0, :], -1.0, gsm[:, 0, :], MUL, MIN).then_inc(gate_nz, 1)
            dve.wait_ge(gate_nz, n(gate_nz))
            dve.wait_ge(gate_ln, 1)
            stt(gsm[:, 6, :], gsm[:, 0, :], 0.0, gsm[:, 3, :], MAX, ADD).then_inc(vec_step, 1)
            dve.wait_ge(vec_step, n(vec_step))
            dve.wait_ge(gate_ea, 1)
            stt(gsm[:, 5, :], gsm[:, 6, :], -1.0, gsm[:, 4, :], MUL, MUL).then_inc(g_ready, 1)
            dve.wait_ge(g_ready, n(g_ready))
            dve.wait_ge(gc_done, 1)
            copy(gcl.rearrange("p z n -> p (z n)"), PS[:, 4, 0:32]).then_inc(vec_step, 1)
            dve.wait_ge(vec_step, n(vec_step))
            tt(g3[:, 0, :], gcl[:, 1, :], gcl[:, 0, :], SUB).then_inc(vec_step, 1)
            dve.wait_ge(vec_step, n(vec_step))
            copy(g3[:, 1:3, :].rearrange("p z n -> p (z n)"), gcl.rearrange("p z n -> p (z n)")).then_inc(e3_in, 1)
            dve.wait_ge(e3_in, n(e3_in))
            dve.wait_ge(e3_ready, 1)
            dve.wait_ge(gate_sg, 1)
            beta = sgm[:, :, 0:NH]
            tt(kb.rearrange("p (c h) -> p c h", h=NH), e3[:, 1, :].rearrange("p (c h) -> p c h", h=NH), beta, MUL).then_inc(vec_step, 1)
            dve.wait_ge(vec_step, n(vec_step))

            def head_norm(t, dst, gain, width=S):
                dve.wait_ge(hs_std, t + 1)
                r = rs[:, t % 2, :width]
                V.reciprocal(r, r).then_inc(vec_step, 1)
                dve.wait_ge(vec_step, n(vec_step))
                stt(dst, dst, gain, r, MUL, MUL).then_inc(hs_normed, 1)
                dve.wait_ge(hs_normed, n(hs_normed))

            for t in range(14):
                dst = qkv[:, t, :] if t < 8 else (mix[:, t - 4, :] if t < 12 else kswn[:, t - 12, :])
                gain = SCALE if t < 4 else 1.0 if t < 8 else par("qnorm") if t < 12 else par("kn_slc" if t == 12 else "kn_win")
                head_norm(t, dst, gain)
            upper, strict = cst("upper"), cst("strict")
            for h in range(NH):
                tt(Ug[:, h], mid(upper, NC), last(gsm[:, 5, h::NH], P), MUL).then_inc(ug_ready if h == NH - 1 else vec_step, 1)
                dve.wait_ge(ug_ready if h == NH - 1 else vec_step, n(ug_ready if h == NH - 1 else vec_step))
            for h in range(NH):
                tt(Ib[:, h], mid(ident, NC), last(beta[:, :, h], P), MUL).then_inc(ug_ready if h == NH - 1 else vec_step, 1)
                dve.wait_ge(ug_ready if h == NH - 1 else vec_step, n(ug_ready if h == NH - 1 else vec_step))
            for h in range(NH):
                b = 4 * (h % 2)
                dve.wait_ge(prep_ps, h + 1)
                d, m = t1[:, h % 2, :], t2[:, h % 2, :]
                d3, m3 = (v.rearrange("p (c n) -> p c n", n=P) for v in (d, m))
                tt(d3, PS[:, b, :].rearrange("p (c n) -> p c n", n=P), last(gcl[:, 0, h::NH], P), SUB).then_inc(vec_step, 1)
                dve.wait_ge(vec_step, n(vec_step))
                ts(d, d, 0.0, None, MIN, ALU.bypass).then_inc(dec_in, 1)
                dve.wait_ge(dec_in, n(dec_in))
                tt(m3, PS[:, b + 1, :].rearrange("p (c n) -> p c n", n=P), mid(strict, NC), MUL).then_inc(vec_step, 1)
                dve.wait_ge(vec_step, n(vec_step))
                dve.wait_ge(eg_ready, h + 1)
                tt(qdT[:, h, :], qkv[:, h, :], eg, MUL).then_inc(vec_step, 1)
                dve.wait_ge(vec_step, n(vec_step))
                dve.wait_ge(dec_exp, h + 1)
                tt(d3, d3, mid(upper, NC), MUL).then_inc(vec_step, 1)
                dve.wait_ge(vec_step, n(vec_step))
                tt(flat(attnT[:, h]), PS[:, b + 3, :], d, MUL).then_inc(vec_step, 1)
                dve.wait_ge(vec_step, n(vec_step))
                tt(d, PS[:, b + 2, :], d, MUL).then_inc(vec_step, 1)
                dve.wait_ge(vec_step, n(vec_step))
                tt(flat(At[:, h]), d, m, MUL).then_inc(prep_done, 1)
                dve.wait_ge(prep_done, n(prep_done))
            for t in range(8):
                dve.wait_ge(tr_ready, t + 1)
                h = t % NH
                src = PS[:, t % 2, :].rearrange("p (c n) -> p c n", n=P)
                if t < NH:
                    tt(kd[:, h], src, last(e3[:, 0, h::NH], P), MUL).then_inc(vec_step, 1)
                    dve.wait_ge(vec_step, n(vec_step))
                    tt(kbg[:, h], src, last(kb[:, h::NH], P), MUL).then_inc(kv_done, 1)
                    dve.wait_ge(kv_done, n(kv_done))
                else:
                    tt(vb[:, h], src, last(beta[:, :, h], P), MUL).then_inc(kv_done, 1)
                    dve.wait_ge(kv_done, n(kv_done))

            def level(h, lv):
                b = CONST["levels"][0]
                mask = const[:, b:b + P] if isinstance(lv, int) and lv == 0 else const[:, bass.ds(lv * P + b, P)]
                tt(Am[:, h], At[:, h], mid(mask, NC), MUL).then_inc(am_ready, 1)
                dve.wait_ge(am_ready, n(am_ready))

            def update(h, i):
                dve.wait_ge(pq_done, i * NH + h + 1)
                tt(flat(Tm[:, h]), flat(Tm[:, h]), PS[:, 2 + h % 2, :], SUB).then_inc(vec_step, 1)
                dve.wait_ge(vec_step, n(vec_step))
                tt(flat(TT[:, h]), flat(TT[:, h]), PS[:, 4 + h % 2, :], SUB).then_inc(tt_ready, 1)
                dve.wait_ge(tt_ready, n(tt_ready))

            for h in range(NH):
                tt(Tm[:, h], mid(ident, NC), mid(ones, NC), MUL).then_inc(vec_step, 1)
                dve.wait_ge(vec_step, n(vec_step))
                tt(TT[:, h], mid(ident, NC), mid(ones, NC), MUL).then_inc(tt_ready, 1)
                dve.wait_ge(tt_ready, n(tt_ready))
                level(h, 0)
            with dve.Fori(0, LEVELS - 1) as i:
                n.enter(i, (tt_ready, NH), (am_ready, NH), (vec_step, NH))
                for h in range(NH):
                    update(h, i)
                    level(h, i + 1)
                n.leave(LEVELS - 1)
            for h in range(NH):
                update(h, LEVELS - 1)
            for h in range(NH):
                dve.wait_ge(uw_done, h + 1)
                copy(flat(wT[:, h]), PS[:, 2 * (h % 2) + 1, :]).then_inc(w_ready, 1)
                dve.wait_ge(w_ready, n(w_ready))
            V.memset(Sst, 0.0).then_inc(state_ready, 1)
            dve.wait_ge(state_ready, n(state_ready))
            for c in range(NC):
                dve.wait_ge(ws_done, c + 1)
                if c == 0:
                    dve.wait_ge(u_ready, NH)
                tt(vn, Um[:, :, c, :], PS[:, 0, :].rearrange("p (h n) -> p h n", n=P), SUB).then_inc(vnew_ready, 1)
                dve.wait_ge(vnew_ready, n(vnew_ready))
                dve.wait_ge(s_done, c + 1)
                for h in range(NH):
                    stt(Sst[:, h, :], Sst[:, h, :], e3[:, 2, c * NH + h:c * NH + h + 1], PS[:, 3, h * P:(h + 1) * P], MUL, ADD).then_inc(state_ready, 1)
                    dve.wait_ge(state_ready, n(state_ready))
            for h in range(NH):
                head_norm(14 + h, oT[:, h, :], par("onorm"))
                tt(mix[:, h, :], mix[:, h, :], oT[:, h, :], MUL).then_inc(og_ready, 1)
                dve.wait_ge(og_ready, n(og_ready))
            for z in range(2):
                k_ = kcvc[:, z, :]
                win = bass.AP(k_.tensor, k_.offset, [list(k_.ap[0]), [1, CMP_L], [CMP_STRIDE, NCMP]])
                tt(kcp[:, z], win, last(par("pos_k" if z == 0 else "pos_v", 0, CMP_L), NCMP), ADD).then_inc(kcp_ready, 1)
                dve.wait_ge(kcp_ready, n(kcp_ready))
            dve.wait_ge(kc_ready, 1)
            head_norm(18, kct[:, :NCMP], par("kn_cmp"), NCMP)
            cneg = cst("cmpneg").rearrange("p (c n) -> p c n", n=NCMP)
            cmask = cst("cmpmask").rearrange("p (c n) -> p c n", n=NCMP)

            def prep(t):
                c, h = divmod(t, NH)
                N = (c + 1) * P
                m = mx[:, t % 2, :]
                dve.wait_ge(sc_done, t + 1)
                both = PS[:, 2 * (t % 2):2 * (t % 2) + 2, :N]
                tt(both[:, :, c * P:], both[:, :, c * P:], mid(cst("causal"), 2), ADD).then_inc(vec_step, 1)
                dve.wait_ge(vec_step, n(vec_step))
                tt(sc[:, t % 2, :NCMP], PS[:, 4 + t % 2, :NCMP], cneg[:, c, :], ADD).then_inc(vec_step, 1)
                dve.wait_ge(vec_step, n(vec_step))
                V.tensor_reduce(m[:, 1:3], both, X, MAX).then_inc(vec_step, 1)
                dve.wait_ge(vec_step, n(vec_step))
                V.tensor_reduce(m[:, 0:1], sc[:, t % 2, :NCMP], X, MAX).then_inc(vec_step, 1)
                dve.wait_ge(vec_step, n(vec_step))
                ts(sc[:, t % 2, :NCMP], sc[:, t % 2, :NCMP], m[:, 0:1], None, SUB, ALU.bypass).then_inc(vec_step, 1)
                dve.wait_ge(vec_step, n(vec_step))
                ts(m[:, 4:6], m[:, 1:3], -SCALE, None, MUL, ALU.bypass).then_inc(negm_ready, 1)
                dve.wait_ge(negm_ready, n(negm_ready))

            prep(0)
            for t in range(NC * NH):
                c, h = divmod(t, NH)
                N = (c + 1) * P
                m = mx[:, t % 2, :]
                if t + 1 < NC * NH:
                    prep(t + 1)
                dve.wait_ge(p_ready, 3 * (t + 1))
                V.reciprocal(m[:, 9:12], m[:, 6:9]).then_inc(vec_step, 1)
                dve.wait_ge(vec_step, n(vec_step))
                tt(m[:, 12:15], m[:, 9:12], sgm[:, c, NH + 3 * h:NH + 3 * h + 3], MUL).then_inc(vec_step, 1)
                dve.wait_ge(vec_step, n(vec_step))
                stt(Pc[:, t % 2, :NCMP], Pc[:, t % 2, :NCMP], m[:, 12:13], cmask[:, c, :], MUL, MUL).then_inc(pn_ready, 1)
                dve.wait_ge(pn_ready, n(pn_ready))
                ts(Pm[:, t % 2, 0, :N], Pm[:, t % 2, 0, :N], m[:, 13:14], None, MUL, ALU.bypass).then_inc(pn_ready, 1)
                dve.wait_ge(pn_ready, n(pn_ready))
                ts(Pm[:, t % 2, 1, :N], Pm[:, t % 2, 1, :N], m[:, 14:15], None, MUL, ALU.bypass).then_inc(pn_ready, 1)
                dve.wait_ge(pn_ready, n(pn_ready))
                dve.wait_ge(pt_done, t + 1)
                if t >= 2:
                    dve.wait_ge(av_done, t - 1)
                copy(PT[:, t % 2, 4:5 + c, :], PS[:, 7, :N].rearrange("p (k q) -> p k q", q=P)).then_inc(pt_vec, 1)
                dve.wait_ge(pt_vec, n(pt_vec))

            def residual(name, blk, col, ready, blocks=1):
                for m in range(KT):
                    dve.wait_ge(blocks_done, FIRST[name] + blocks * (m + 1))
                    stt(xT[:, m, :], PS[:, m % 4, :], mod[:, blk, col + m:col + m + 1], xT[:, m, :], MUL, ADD).then_inc(ready, 1)
                    dve.wait_ge(ready, n(ready))

            residual("w_out", 0, 16, x1_ready)
            norm(1)
            with dve.Fori(0, FT // 2) as i:
                n.enter(i, (fy_ready, 4), (ff_ready, 2), (vec_step, 8))
                for u in range(2):
                    for z in range(2):
                        j = 2 * u + z
                        dve.wait_ge(blocks_done, FIRST["up"] + i * 4 + j + 1)

                        def tap(s_):
                            return param[:, bass.ds(i * 12 + (PARAM["fconv"][0] + 3 * j + s_), 1)]
                        o = (y0 if z == 0 else y1)[:, u, :]
                        ts(o, PS[:, j, :], tap(2), param[:, bass.ds(i * 4 + (PARAM["fbias"][0] + j), 1)], MUL, ADD).then_inc(vec_step, 1)
                        dve.wait_ge(vec_step, n(vec_step))
                        for s_ in (1, 2):
                            stt(o[:, s_:], PS[:, j, :S - s_], tap(2 - s_), o[:, s_:], MUL, ADD).then_inc(fy_ready if s_ == 2 else vec_step, 1)
                            dve.wait_ge(fy_ready if s_ == 2 else vec_step, n(fy_ready if s_ == 2 else vec_step))
                    dve.wait_ge(sa_ready, i * 2 + u + 1)
                    tt(gT[:, bass.ds(i * 2 + u, 1), :].rearrange("p o n -> p (o n)"), sa[:, u, :], y1[:, u, :], MUL).then_inc(ff_ready, 1)
                    dve.wait_ge(ff_ready, n(ff_ready))
                n.leave(FT // 2)
            residual("down", 0, 40, x2_ready, 2)
            norm(2)
            V.memset(pT[:, :, :16], 0.0).then_inc(vec_step, 1)
            dve.wait_ge(vec_step, n(vec_step))
            V.memset(glu[:, :, :30], 0.0).then_inc(vec_step, 1)
            dve.wait_ge(vec_step, n(vec_step))
            V.memset(cs1[:, :16], 0.0).then_inc(vec_step, 1)
            dve.wait_ge(vec_step, n(vec_step))
            V.memset(cs2[:, :16], 0.0).then_inc(vec_step, 1)
            dve.wait_ge(vec_step, n(vec_step))
            cnt = cst("poolcnt").rearrange("p (g n) -> p g n", n=16)
            for g in range(4):
                dve.wait_ge(sg_ready, g + 1)
                src = pT[:, g, :]
                for s_ in range(g + 1):
                    dst = (cs1, cs2)[s_ % 2]
                    d_ = 1 << s_
                    tt(dst[:, 16:], src[:, 16:], src[:, 16 - d_:16 + S - d_], ADD).then_inc(vec_step, 1)
                    dve.wait_ge(vec_step, n(vec_step))
                    src = dst
                w = PW[g]
                tt(src[:, 16:16 + w], src[:, 16:16 + w], cnt[:, g, :w], MUL).then_inc(vec_step, 1)
                dve.wait_ge(vec_step, n(vec_step))
                stt(mx4[:, g, :w], pT[:, g, 16:16 + w], -1.0, src[:, 16:16 + w], MUL, ADD).then_inc(vec_step, 1)
                dve.wait_ge(vec_step, n(vec_step))
                stt(mx4[:, g, w:], src[:, 16 + w:], 1.0 / w, pT[:, g, 16 + w:], MUL, SUB).then_inc(pm_ready, 1)
                dve.wait_ge(pm_ready, n(pm_ready))
            for t in range(4):
                dve.wait_ge(sg_ready, 4 + 2 * t + 2)
                tt(glu[:, t, 30:], a1[:, t % 2, :], a2[:, t % 2, :], MUL).then_inc(glu_ready, 1)
                dve.wait_ge(glu_ready, n(glu_ready))
            for t in range(4):
                ts(yc[:, t, :], glu[:, t, 30:], par("dw", t * TAPS + TAPS - 1), par("dwb", t), MUL, ADD).then_inc(vec_step, 1)
                dve.wait_ge(vec_step, n(vec_step))
            for s_ in range(1, TAPS):
                for t in range(4):
                    stt(yc[:, t, :], glu[:, t, 30 - s_:30 - s_ + S], par("dw", t * TAPS + TAPS - 1 - s_), yc[:, t, :], MUL, ADD).then_inc(ln_in if s_ == TAPS - 1 and t == 3 else vec_step, 1)
                    dve.wait_ge(ln_in if s_ == TAPS - 1 and t == 3 else vec_step, n(ln_in if s_ == TAPS - 1 and t == 3 else vec_step))
            dve.wait_ge(ln_mu, 1)
            for g in range(4):
                tt(yc[:, g, :], yc[:, g, :], lnm, SUB).then_inc(ln_y, 1)
                dve.wait_ge(ln_y, n(ln_y))
            dve.wait_ge(ln_std, 1)
            V.reciprocal(rs[:, 0, :], rs[:, 0, :]).then_inc(vec_step, 1)
            dve.wait_ge(vec_step, n(vec_step))
            for g in range(4):
                tt(yc[:, g, :], yc[:, g, :], rs[:, 0, :], MUL).then_inc(vec_step, 1)
                dve.wait_ge(vec_step, n(vec_step))
                ts(yc[:, g, :], yc[:, g, :], par("lng", g), par("lnb", g), MUL, ADD).then_inc(ln_y, 1)
                dve.wait_ge(ln_y, n(ln_y))
            for m in range(KT):
                dve.wait_ge(blocks_done, FIRST["branch"] + m + 1)
                b = 2 * (m % 2)
                tt(m1[:, 0, :], PS[:, b, :], sgT[:, m, :], MUL).then_inc(vec_step, 1)
                dve.wait_ge(vec_step, n(vec_step))
                tt(m1[:, 1, :], PS[:, b + 1, :], sgT[:, 8 + m, :], MUL).then_inc(m_half, 1)
                dve.wait_ge(m_half, n(m_half))
                tt(mg[:, m, :], m1[:, 0, :], m1[:, 1, :], ADD).then_inc(merged, 1)
                dve.wait_ge(merged, n(merged))
            residual("w_out_2", 1, 16, x3_ready)
            norm(3)
            for t in range(2 * NC):
                c, half = divmod(t, 2)
                dve.wait_ge(hr_done, t + 1)
                copy(hrow[:, c, half * S:(half + 1) * S], PS[:, 4 + t % 2, :]).then_inc(hr_ready, 1)
                dve.wait_ge(hr_ready, n(hr_ready))
            iota = cst("iota")

            def top16(src, val, ind, scratch):
                V.max(val[:, 0:8], src).then_inc(vec_step, 1)
                dve.wait_ge(vec_step, n(vec_step))
                V.max_index(ind[:, 0:8], val[:, 0:8], src).then_inc(vec_step, 1)
                dve.wait_ge(vec_step, n(vec_step))
                V.match_replace(scratch, val[:, 0:8], src, NEG).then_inc(vec_step, 1)
                dve.wait_ge(vec_step, n(vec_step))
                V.max(val[:, 8:16], scratch).then_inc(vec_step, 1)
                dve.wait_ge(vec_step, n(vec_step))
                V.max_index(ind[:, 8:16], val[:, 8:16], scratch).then_inc(vec_step, 1)
                dve.wait_ge(vec_step, n(vec_step))

            for c in range(NC):
                for j in range(16):
                    dve.wait_ge(sc2_ready, 4 * c + j // 4 + 1)
                    top16(sS[:, j, :], vals[:, j, :], idx[:, j, :], s2[:, 0, :NKEYS])
                copy(idf.rearrange("p j k -> p (j k)"), idx[:].rearrange("p j k -> p (j k)")).then_inc(vec_step, 1)
                dve.wait_ge(vec_step, n(vec_step))
                v4 = vals.rearrange("p (h z) k -> p h z k", z=2)
                i4 = idf.rearrange("p (h z) k -> p h z k", z=2)
                for h in range(HEADS):
                    tt(cand[:, h, :].rearrange("p (x y) -> p x y", y=16), last(v4[:, h, 0, :], 16), mid(v4[:, h, 1, :], 16), ADD).then_inc(vec_step, 1)
                    dve.wait_ge(vec_step, n(vec_step))
                    top16(cand[:, h, :], tops[:, h, :], pos[:, 0, h * 16:(h + 1) * 16], s2[:, 1, :])
                V.tensor_scalar(pos[:, 1, :], pos[:, 0, :], 4, None, ALU.logical_shift_right).then_inc(vec_step, 1)
                dve.wait_ge(vec_step, n(vec_step))
                V.tensor_scalar(pos[:, 2, :], pos[:, 0, :], 15, None, ALU.bitwise_and).then_inc(vec_step, 1)
                dve.wait_ge(vec_step, n(vec_step))
                for z in range(2):
                    copy(ifl[:, z, :], pos[:, 1 + z, :]).then_inc(vec_step, 1)
                    dve.wait_ge(vec_step, n(vec_step))
                    tt(eqv, last(ifl[:, z, :].rearrange("p (h k) -> p h k", k=16), 16), mid(iota, HEADS, 16), ALU.is_equal).then_inc(vec_step, 1)
                    dve.wait_ge(vec_step, n(vec_step))
                    for h in range(HEADS):
                        tt(eqv[:, h], eqv[:, h], mid(i4[:, h, z, :], 16), MUL).then_inc(vec_step, 1)
                        dve.wait_ge(vec_step, n(vec_step))
                    V.tensor_reduce(ifl[:, 2 + z, :], eqv.rearrange("p h k x -> p (h k) x"), X, ADD).then_inc(vec_step, 1)
                    dve.wait_ge(vec_step, n(vec_step))
                stt(ifl[:, 0, :], ifl[:, 2, :], float(NKEYS), ifl[:, 3, :], MUL, ADD).then_inc(vec_step, 1)
                dve.wait_ge(vec_step, n(vec_step))
                copy(expi[:, c * HEADS:(c + 1) * HEADS, :].rearrange("p h k -> p (h k)"), ifl[:, 0, :]).then_inc(vec_step, 1)
                dve.wait_ge(vec_step, n(vec_step))
                tt(gate[:, c], tops, last(tops[:, :, 0], 16), SUB).then_inc(sm_in, 1)
                dve.wait_ge(sm_in, n(sm_in))
                dve.wait_ge(sm_exp, c + 1)
                V.tensor_reduce(sm[:, 0, :HEADS], gate[:, c], X, ADD).then_inc(vec_step, 1)
                dve.wait_ge(vec_step, n(vec_step))
                V.reciprocal(sm[:, 1, :HEADS], sm[:, 0, :HEADS]).then_inc(vec_step, 1)
                dve.wait_ge(vec_step, n(vec_step))
                tt(gate[:, c], gate[:, c], last(sm[:, 1, :HEADS], 16), MUL).then_inc(routed, 1)
                dve.wait_ge(routed, n(routed))
            V.memset(expi[:, NC * HEADS, :], 0).then_inc(vec_step, 1)
            dve.wait_ge(vec_step, n(vec_step))
            for u in range(2):
                copy(ecur[:, u, :], expi[:, 0, u * RING:(u + 1) * RING]).then_inc(ecur_ready, 1)
                dve.wait_ge(ecur_ready, n(ecur_ready))
            for c in range(NC):
                with dve.Fori(0, HEADS) as h:
                    n.enter(h, (dots_ready, 16), (ecur_ready, 2))
                    for u in range(2):
                        for r in range(RING):
                            dve.wait_ge(row_landed[r], 16 * (c * 16 + u + 1) + h * 32)
                            b, k = divmod(r, BATCH)
                            V.tensor_tensor_reduce(out=junk, in0=ring_e[:, r, :D], in1=hrow[:, c, :], scale=1.0, scalar=0.0,
                                                       op0=MUL, op1=ADD, accum_out=dots[:, b, k:k + 1]).then_inc(dots_ready, 1)
                            dve.wait_ge(dots_ready, n(dots_ready))
                        V.tensor_copy(ecur[:, u, :], expi[:, bass.ds(h + (c * HEADS + 1), 1), u * RING:(u + 1) * RING].rearrange("p o k -> p (o k)")).then_inc(ecur_ready, 1)
                        dve.wait_ge(ecur_ready, n(ecur_ready))
                    n.leave(HEADS)
                for v in range(2):
                    dve.wait_ge(pt2_done, 2 * c + v + 1)
                    for k in range(4):
                        m = 4 * v + k
                        o = xT[:, m, c * P:(c + 1) * P]
                        stt(o, PS[:, 2 + v, k * P:(k + 1) * P], mod[:, 1, 40 + m:41 + m], o, MUL, ADD).then_inc(x4_ready, 1)
                        dve.wait_ge(x4_ready, n(x4_ready))
            norm(4)

        @block.gpsimd
        def _(pool):
            def rows(p, u, first=False):
                pool.wait_ge(ecur_ready, p + 1)
                pool.sem_inc(pool_seen, 1)
                for r in range(RING):
                    if not first and r % BATCH == 0:
                        pool.wait_ge(rows_used, p * 2 + (r // BATCH - 1))
                        pool.sem_inc(pool_seen, 1)
                    nc.gpsimd.indirect_dma_start(
                        out=ring_e[:, r, :], out_offset=None, in_=a["experts"],
                        in_offset=bass.IndirectOffsetOnAxis(ap=ecur[:, u, r:r + 1], axis=0)
                    ).then_inc(row_landed[r], 16)

            rows(0, 0, True)
            with pool.Fori(0, 2 * HEADS * NC // 2 - 1) as i:
                rows(i * 2 + 1, 1)
                rows(i * 2 + 2, 0)
            rows(2 * HEADS * NC - 1, 1)


def tiles_of(w):
    k, n = w.shape
    return np.ascontiguousarray(w.reshape(k // P, P, n // P, P).transpose(2, 1, 0, 3).reshape(n // P, P, k))


def rows_of(w):
    k, n = w.shape
    return np.ascontiguousarray(w.reshape(4, 2, P, n // S, S).transpose(3, 0, 2, 1, 4).reshape(-1, P, 2 * S))


def cols(v):
    return np.asarray(v).reshape(-1, P).T


def constants():
    c = np.zeros((P, NCONST), np.float32)
    i = np.arange(P)

    def put(name, v):
        c[:, CONST[name][0]:CONST[name][1]] = np.asarray(v).reshape(P, -1)

    put("ident", np.eye(P))
    put("ones", np.ones((P, P)))
    put("upper", i[:, None] <= i[None, :])
    put("strict", i[:, None] < i[None, :])
    put("causal", np.where(i[None, :] <= i[:, None], 0.0, NEG))
    lv = []
    for l in range(LEVELS):
        b = 1 << l
        same = i[:, None] // (2 * b) == i[None, :] // (2 * b)
        lv.append(same & ((i[:, None] // b) % 2 == 0) & ((i[None, :] // b) % 2 == 1))
    put("levels", np.stack(lv, 1))
    t = np.arange(NC)[None, :, None] * P + i[:, None, None]
    seen = np.arange(NCMP)[None, None, :] * CMP_STRIDE + CMP_L - 1 <= t
    put("cmpneg", np.where(seen, 0.0, NEG))
    put("cmpmask", seen)
    cnt = np.stack([1.0 / np.minimum(np.arange(1, 17), w) for w in PW])
    put("poolcnt", np.broadcast_to(cnt[None], (P, 4, 16)))
    put("iota", np.broadcast_to(np.arange(16.0), (P, 16)))
    put("eps", np.full((P, 1), EPS))
    put("one", np.ones((P, 1)))
    return c


def layout(i):
    g = {k: np.asarray(v) for k, v in i.items()}
    a = {"const": constants()}
    a["x"] = np.ascontiguousarray(g["x"][0].T.reshape(KT, P, S).transpose(1, 0, 2))
    w = g["w_in"][0]
    W4 = NH * HD
    at = np.cumsum([0, W4, W4, W4, W4, NH, NH, W4] + [HD] * 6 + [3 * NH])
    part = [w[:, at[n]:at[n + 1]] for n in range(14)]
    a["w_in"] = tiles_of(np.concatenate([part[n] for n in (0, 1, 2, 3, 6, 7, 8, 9, 11)], 1))
    rw = np.concatenate([part[n] for n in (10, 12, 4, 5, 13)], 1)
    a["roww"] = np.ascontiguousarray(rw.reshape(KT, P, NROW).transpose(1, 0, 2))
    a["ada"], a["ada_2"] = rows_of(g["ada_w"][0]), rows_of(g["ada_w_2"][0])
    a["cmp"] = np.ascontiguousarray(np.stack([g["cmp_k_w1"][0], g["cmp_v_w1"][0]])
                                    .reshape(8, KT, P, P).transpose(0, 2, 1, 3).reshape(8, P, D))
    a["w_out"], a["w_out_2"], a["query"] = tiles_of(g["w_out"][0]), tiles_of(g["w_out_2"][0]), tiles_of(g["w_query_2"][0])
    up = tiles_of(g["ffn_w_up"][0])
    pair = np.arange(2 * FT).reshape(2, FT).T.ravel()
    a["up"] = np.ascontiguousarray(up[pair])
    a["down"] = np.ascontiguousarray(tiles_of(g["ffn_w_down"][0]).reshape(KT, P, 2, WIDE).transpose(0, 2, 1, 3).reshape(16, P, WIDE))
    order = np.array([0, 1, 2, 3, 4, 8, 5, 9, 6, 10, 7, 11] + list(range(12, 28)))
    a["w_in_2"] = np.ascontiguousarray(tiles_of(g["w_in_2"][0])[order])
    a["branch"] = np.ascontiguousarray(np.concatenate([tiles_of(g["pool_up_2"][0]), tiles_of(g["conv_out_2"][0])], 2))
    a["experts"] = np.concatenate([g["expert_u_2"][0], g["expert_v_2"][0]], 1)
    m = np.zeros((P, NMATS), np.float32)
    for n, v in (("w2k", g["cmp_k_w2"][0]), ("w2v", g["cmp_v_w2"][0]), ("keys1", g["sub_keys_1_2"][0].T),
                 ("keys2", g["sub_keys_2_2"][0].T), ("poolw", g["pool_w_2"][0].transpose(1, 0, 2).reshape(P, -1))):
        m[:, MATS[n][0]:MATS[n][1]] = v
    a["mats"] = m
    p = np.zeros((P, NPARAM), np.float32)

    def put(name, v):
        p[:, PARAM[name][0]:PARAM[name][1]] = v

    put("c", cols(g["c"][0])); put("c_2", cols(g["c_2"][0]))
    put("ada_b", cols(g["ada_b"][0])); put("ada_b_2", cols(g["ada_b_2"][0]))
    put("norm1", cols(g["norm1_w"][0])); put("norm2", cols(g["norm2_w"][0]))
    put("norm1_2", cols(g["norm1_g_2"][0])); put("norm2_2", cols(g["norm2_g_2"][0])); put("final", cols(g["final_g_2"]))
    put("gconv", g["gdn_conv_w"][0].reshape(4, 12, P).transpose(2, 1, 0).reshape(P, -1))
    put("a_log", np.broadcast_to(np.tile(g["gdn_A_log"][0], NC), (P, 16)))
    put("dt", np.broadcast_to(np.tile(g["gdn_dt_bias"][0], NC), (P, 16)))
    for n, k in (("onorm", "gdn_out_norm_w"), ("qnorm", "nsa_q_norm_w"), ("kn_cmp", "nsa_k_norm_cmp"),
                 ("kn_slc", "nsa_k_norm_slc"), ("kn_win", "nsa_k_norm_win")):
        put(n, cols(g[k][0]))
    put("pos_k", g["cmp_k_pos"][0].T); put("pos_v", g["cmp_v_pos"][0].T)
    put("fconv", g["ffn_conv_w"][0].reshape(3, 2 * FT, P)[:, pair].transpose(2, 1, 0).reshape(P, -1))
    put("fbias", cols(g["ffn_conv_b"][0])[:, pair])
    put("b_in", cols(g["b_in_2"][0])[:, order])
    put("pscale", cols(g["pool_scale_2"][0]))
    put("dw", g["dw_kernel_2"][0].reshape(TAPS, 4, P).transpose(2, 1, 0).reshape(P, -1))
    put("dwb", cols(g["dw_bias_2"][0])); put("lng", cols(g["conv_ln_g_2"][0])); put("lnb", cols(g["conv_ln_b_2"][0]))
    a["param"] = p
    return a


def program(nc, arrays):
    aps = {n: nc.dram_tensor(f"{n}_dram", v.shape, F32, kind="ExternalInput").ap() for n, v in arrays.items()}
    out = nc.dram_tensor("out_dram", (P, KT, S), F32, kind="ExternalOutput").ap()
    build(nc, aps, out)


def kernel(**inputs):
    from concourse.bass_utils import run_bass_kernel_spmd
    import concourse.bacc as bacc
    arrays = layout(inputs)
    nc = bacc.Bacc("TRN2", target_bir_lowering=False, num_devices=1)
    program(nc, arrays)
    r = run_bass_kernel_spmd(nc, [{f"{n}_dram": v for n, v in arrays.items()}], core_ids=[0])
    got = r.results[0]["out_dram"]
    return np.ascontiguousarray(got.transpose(2, 1, 0).reshape(1, S, D))
```

```python
import numpy as np
import concourse.bass as bass
from concourse import mybir
from contextlib import ExitStack

F32 = mybir.dt.float32
U32 = mybir.dt.uint32
ALU = mybir.AluOpType
ACT = mybir.ActivationFunctionType
X = mybir.AxisListType.X

P = 128
S = 512
D = 1024
KT = D // P
NC = S // P
NH = 4
HD = 128
SCALE = HD ** -0.5
EPS = 1e-6
NEG = -1e30
NCMP = (S - 32) // 16 + 1
CMP_L, CMP_STRIDE = 32, 16
FF = 2816
FT = FF // P
SLOTS = 4
WIDE = FF // 2
LEVELS = 7
MANY = 14
NROW = 2 * HD + 2 * NH + 3 * NH
TAPS = 31
PW = (2, 4, 8, 16)
HEADS, TOPK, NKEYS = 8, 16, 128
RING = 8
BATCH = 2
NB = RING // BATCH
STEPS = NC * HEADS
SB = TOPK // BATCH

def _cols(widths):
    out, at = {}, 0
    for name, w in widths:
        out[name] = (at, at + w)
        at += w
    return out, at

CONST, NCONST = _cols([
    ("ident", P), ("ones", P), ("upper", P), ("strict", P), ("causal", P), ("levels", LEVELS * P),
    ("cmpneg", NC * NCMP), ("cmpmask", NC * NCMP), ("poolcnt", 4 * 16), ("iota", 16), ("strip", 2 * MANY - 1), ("hscale", 1), ("eps", 1), ("one", 1)])
PARAM, NPARAM = _cols([
    ("c", KT), ("c_2", KT), ("ada_b", 48), ("ada_b_2", 48), ("norm1", KT), ("norm2", KT), ("norm1_2", KT),
    ("norm2_2", KT), ("final", KT), ("gconv", 12 * 4), ("a_log", 16), ("dt", 16), ("onorm", 1), ("qnorm", 1),
    ("kn_cmp", 1), ("kn_slc", 1), ("kn_win", 1), ("pos_k", CMP_L), ("pos_v", CMP_L), ("fconv", 2 * FT * 3),
    ("fbias", 2 * FT), ("b_in", 28), ("pscale", 4), ("dw", 4 * TAPS), ("dwb", 4), ("lng", 4), ("lnb", 4)])
MATS, NMATS = _cols([("w2k", P), ("w2v", P), ("keys1", P), ("keys2", P), ("poolw", 4 * P)])
STREAM = [("ada", 48, D), ("w_in", 24, D), ("cmp", 8, D), ("w_out", 8, D), ("up", 2 * FT, D),
          ("down", 16, WIDE), ("w_in_2", 28, D), ("branch", 8, D), ("w_out_2", 8, D), ("query", 16, D)]
FIRST = {}
_at = 0
for _n, _b, _w in STREAM:
    FIRST[_n] = _at
    _at += _b


class Count:

    def __init__(self):
        self.n, self.off, self.per = {}, {}, []

    def __call__(self, sem):
        k = id(sem)
        self.n[k] = self.n.get(k, 0) + 1
        return self.n[k] + self.off.get(k, 0)

    def enter(self, i, *per):
        self.per = [(id(s), v) for s, v in per]
        self.at = dict(self.n)
        self.off = {k: i * v for k, v in self.per}

    def leave(self, passes):
        per = dict(self.per)
        for k, v in self.n.items():
            got = v - self.at.get(k, 0)
            assert got == per.get(k, 0), got
            self.n[k] = self.at.get(k, 0) + got * passes
        self.off, self.per = {}, []


def build(nc, a, out):
    ctx = ExitStack()
    with ctx:
        def sb(name, shape, dt=F32):
            return ctx.enter_context(nc.sbuf_tensor(name, shape, dt))

        xT = sb("xT", [P, KT, S])
        hT = sb("hT", [P, KT, S])
        ring = sb("ring", [P, SLOTS, WIDE])
        const = sb("const", [P, NCONST])
        param = sb("param", [P, NPARAM])
        mats = sb("mats", [P, NMATS])
        sq = sb("sq", [P, 2, S])
        rs = sb("rs", [P, 2, S])
        mod = sb("mod", [P, 2, 48])
        eff = sb("eff", [P, 4, KT])
        silc = sb("silc", [P, 2, KT])
        AR = 32320
        arena = sb("arena", [P, AR])

        def area(at, *dims):
            n = int(np.prod(dims))
            assert at + n <= AR, (at, n)
            v = arena[:, at:at + n]
            names = "abcd"[:len(dims)]
            if len(dims) == 1:
                return v
            return v.rearrange("p (" + " ".join(names) + ") -> p " + " ".join(names),
                               **dict(zip(names[1:], dims[1:])))

        def cst(name):
            return const[:, CONST[name][0]:CONST[name][1]]

        def par(name, i=0, n=1):
            b = PARAM[name][0] + i
            return param[:, b:b + n]

        def mat(name):
            return mats[:, MATS[name][0]:MATS[name][1]]

        ident, ones, eps, one = cst("ident"), cst("ones"), cst("eps"), cst("one")

        acc = area(0, 12, S)
        qkv = area(0, 12, S)
        mix = area(6144, 8, S)
        kcvc = area(10240, 2, S)
        kswn = area(11264, 2, S)
        vrow = area(12288, NC, 2, HD)
        roww = area(13312, KT, NROW)
        cv = area(15520, 2, S)
        small = area(16544, NC, 20)
        sgm = area(16624, NC, 16)
        gsm = area(16688, 8, 16)
        g3 = area(16816, 3, 16)
        e3 = area(16864, 3, 16)
        kb = area(16912, 16)
        gcl = area(16928, 2, 16)
        Tm = area(2048, NH, NC, P)
        TT = area(0, NH, NC, P)
        Am = area(4096, NH, NC, P)
        Y = area(13312, NH, NC, P)
        select = area(25152, MANY, P)
        t1 = area(16960, 2, S)
        t2 = area(17984, 2, S)
        kbg = area(19008, NH, NC, P)
        kd = area(21056, NH, NC, P)
        vb = area(23104, NH, NC, P)
        attnT = area(25152, NH, NC, P)
        At = area(27200, NH, NC, P)
        qdT = area(29248, NH, S)
        Ug = area(19008, NH, NC, P)
        Ib = area(13312, NH, NC, P)
        eg = area(31296, S)
        Sst = area(31296, NH, HD)
        vn = area(31808, NH, HD)
        Um = Tm
        wT = Am
        oT = area(13312, NH, S)
        kcp = area(0, 2, CMP_L, NCMP)
        hid = area(19008, 2, NCMP)
        kct = area(19072, NCMP)
        vcr = area(19104, HD)
        Pm = area(19232, 2, 2, S)
        Pc = area(21280, 2, 32)
        sc = area(21344, 2, 32)
        PT = area(21408, 2, 9, P)
        mx = area(23712, 2, 16)
        gT = area(0, FT, S)
        y0 = area(FT * S, 2, S)
        y1 = area(FT * S + 1024, 2, S)
        sa = area(FT * S + 2048, 2, S)
        acc_2 = area(FT * S + 3072, 12, S)
        ring_2 = area(FT * S + 9216, SLOTS, 2 * S)
        sgT = area(0, 16, S)
        pT = area(8192, 4, 16 + S)
        glu = area(10304, 4, 30 + S)
        a1 = area(12472, 2, S)
        a2 = area(13496, 2, S)
        cs1 = area(14520, 16 + S)
        cs2 = area(15048, 16 + S)
        mx4 = area(15576, 4, S)
        pmT = area(17624, 4, S)
        yc = area(19672, 4, S)
        m1 = area(21720, 2, S)
        mg = area(22744, 8, S)
        lnm = area(26840, S)
        ring_e = area(0, RING, 2 * D)
        qT = area(RING // 2 * 2 * D, 16, S)
        sS = area(16384, STEPS, 2 * NKEYS)
        hrow = area(24576, NC, D)
        scur = area(28672, 2, NKEYS)
        s2 = area(28928, 256)
        vcur = area(29184, 2, 16)
        idf = area(29216, 2, 16)
        cand = area(29248, 256)
        tcur = area(29504, 16)
        ifl = area(29520, 2, 16)
        sel = area(29552, 2, 16)
        eqv = area(29584, 2, 16, 16)
        exf = area(30096, 16)
        gcur = area(30112, 2, 16)
        gsum = area(30144, 2, 2)
        dots = area(30148, NB, BATCH)
        wts = area(30164, NB, BATCH)
        prow = hT[:, 0:2, :].rearrange("p k n -> p (k n)")
        fsq = sq.rearrange("p u n -> p (u n)").rearrange("p (k n) -> p k n", n=P)
        diag = hT[:, 2:4, :].rearrange("p k (b n) -> p (k b) n", n=P).rearrange("p (b k) n -> p b k n", k=BATCH)
        junk = hT[:, 4:6, :].rearrange("p k n -> p (k n)")
        ecur = sb("ecur", [P, 2, TOPK], U32)
        icur = sb("icur", [P, 2, TOPK], U32)
        pcur = sb("pcur", [P, TOPK], U32)
        pab = sb("pab", [P, 2, TOPK], U32)

        PS = ctx.enter_context(nc.psum_tensor("PS", [P, 8, S], F32))

        def sem(name):
            return ctx.enter_context(nc.semaphore(name))

        act_step = sem("act_step")
        ada_2_used = sem("ada_2_used")
        am_ready = sem("am_ready")
        att_ready = sem("att_ready")
        av_done = sem("av_done")
        b_in = sem("b_in")
        blocks_done = sem("blocks_done")
        conv_ready = sem("conv_ready")
        dec_exp = sem("dec_exp")
        dec_in = sem("dec_in")
        diag_ready = sem("diag_ready")
        dots_ready = sem("dots_ready")
        e3_in = sem("e3_in")
        e3_ready = sem("e3_ready")
        ecur_ready = sem("ecur_ready")
        eg_ready = sem("eg_ready")
        ff_ready = sem("ff_ready")
        fin_ready = sem("fin_ready")
        fin_sq = sem("fin_sq")
        fin_std = sem("fin_std")
        fin_sum = sem("fin_sum")
        fy_ready = sem("fy_ready")
        g_ready = sem("g_ready")
        gate_e = sem("gate_e")
        gate_ea = sem("gate_ea")
        gate_ln = sem("gate_ln")
        gate_nz = sem("gate_nz")
        gate_sg = sem("gate_sg")
        gc_done = sem("gc_done")
        gelu_ready = sem("gelu_ready")
        glu_ready = sem("glu_ready")
        h_ready = sem("h_ready")
        hid_ready = sem("hid_ready")
        hr_done = sem("hr_done")
        hr_ready = sem("hr_ready")
        hm_bc = sem("hm_bc")
        hm_normed = sem("hm_normed")
        hm_ready = sem("hm_ready")
        hm_recip = sem("hm_recip")
        hm_std = sem("hm_std")
        hm_used = sem("hm_used")
        hs_normed = sem("hs_normed")
        hs_ready = sem("hs_ready")
        hs_std = sem("hs_std")
        hs_used = sem("hs_used")
        inputs_loaded = sem("inputs_loaded")
        rest_loaded = sem("rest_loaded")
        kc_done = sem("kc_done")
        kc_ready = sem("kc_ready")
        kcp_ready = sem("kcp_ready")
        kv_done = sem("kv_done")
        ln_in = sem("ln_in")
        ln_mu = sem("ln_mu")
        ln_sq = sem("ln_sq")
        ln_std = sem("ln_std")
        ln_sum1 = sem("ln_sum1")
        ln_sum2 = sem("ln_sum2")
        ln_y = sem("ln_y")
        m_half = sem("m_half")
        merged = sem("merged")
        mod_ready = sem("mod_ready")
        modcol_done = sem("modcol_done")
        negm_ready = sem("negm_ready")
        normed = sem("normed")
        o_done = sem("o_done")
        o_ready = sem("o_ready")
        og_ready = sem("og_ready")
        out_done = sem("out_done")
        p_ready = sem("p_ready")
        params_loaded = sem("params_loaded")
        pm_ready = sem("pm_ready")
        pn_ready = sem("pn_ready")
        pool_done = sem("pool_done")
        pool_seen = sem("pool_seen")
        pq_done = sem("pq_done")
        prep_done = sem("prep_done")
        prep_ps = sem("prep_ps")
        prow_ready = sem("prow_ready")
        pscaled = sem("pscaled")
        pt2_done = sem("pt2_done")
        pt_act = sem("pt_act")
        pt_done = sem("pt_done")
        pt_vec = sem("pt_vec")
        q_ready = sem("q_ready")
        qkv_ready = sem("qkv_ready")
        gate_ready = sem("gate_ready")
        row_evac = sem("row_evac")
        rows_done = sem("rows_done")
        rows_used = sem("rows_used")
        s_done = sem("s_done")
        sa_ready = sem("sa_ready")
        sc2_done = sem("sc2_done")
        sc2_ready = sem("sc2_ready")
        sc_done = sem("sc_done")
        sc_ready = sem("sc_ready")
        sc_sub = sem("sc_sub")
        sg_ready = sem("sg_ready")
        silu_c_ready = sem("silu_c_ready")
        sm_exp = sem("sm_exp")
        sm_in = sem("sm_in")
        sq_ready = sem("sq_ready")
        sq_used = sem("sq_used")
        state_ready = sem("state_ready")
        std_ready = sem("std_ready")
        tr_ready = sem("tr_ready")
        tt_ready = sem("tt_ready")
        u_ready = sem("u_ready")
        ug_ready = sem("ug_ready")
        uw_done = sem("uw_done")
        vc_ready = sem("vc_ready")
        vec_seen = sem("vec_seen")
        vec_step = sem("vec_step")
        vnew_ready = sem("vnew_ready")
        w_ready = sem("w_ready")
        w_ready2 = sem("w_ready2")
        ws_done = sem("ws_done")
        x1_ready = sem("x1_ready")
        x2_ready = sem("x2_ready")
        x3_ready = sem("x3_ready")
        x4_ready = sem("x4_ready")
        y_done = sem("y_done")
        y_ready = sem("y_ready")
        yc_ready = sem("yc_ready")
        zq_ready = sem("zq_ready")
        slot_ready = [sem(f"slot{j}_ready") for j in range(SLOTS)]
        slot_2_ready = [sem(f"ada_2_slot{j}_ready") for j in range(SLOTS)]
        row_landed = [sem(f"expert_row{j}_ready") for j in range(RING)]

        block = ctx.enter_context(nc.Block())

        @block.sync
        def _(sp):
            sp.dma_start(param[:], a["param"]).then_inc(params_loaded, 16)
            first = STREAM[0]
            sp.dma_start(const[:], a["const"]).then_inc(inputs_loaded, 16)
            sp.dma_start(xT[:], a["x"]).then_inc(inputs_loaded, 16)
            for j in range(SLOTS):
                sp.dma_start(ring[:, j, :D], a["ada"][j]).then_inc(slot_ready[j], 16)
            sp.dma_start(roww, a["roww"]).then_inc(rest_loaded, 16)
            sp.dma_start(mats[:], a["mats"]).then_inc(rest_loaded, 16)
            sp.dma_start(select[0:MANY], a["select"]).then_inc(rest_loaded, 16)
            for name, blocks, width in STREAM:
                lo = 1 if name == first[0] else 0
                with sp.Fori(lo, blocks // SLOTS) as i:
                    for j in range(SLOTS):
                        sp.wait_ge(blocks_done, FIRST[name] + i * SLOTS + j - SLOTS + 1)
                        sp.dma_start(ring[:, j, :width],
                                     a[name][bass.ds(i * SLOTS + j, 1)].rearrange("o p n -> p (o n)")
                                     ).then_inc(slot_ready[j], 16)
            for c in range(NC):
                sp.wait_ge(fin_ready, c + 1)
                sp.dma_start(out[:, :, c * P:(c + 1) * P], xT[:, :, c * P:(c + 1) * P]).then_inc(out_done, 16)
            sp.wait_ge(out_done, 16 * NC)


        @block.tensor
        def _(pe):
            def mm(o, l, r, start=True, stop=True):
                return nc.tensor.matmul(o, l, r, start=start, stop=stop)

            def tiles(j, n=KT):
                return [ring[:, j, k * P:(k + 1) * P] for k in range(n)]

            def gemm(name, rhs, freed, base, first=0, last=None, h=None):
                last = dict((n, b) for n, b, _ in STREAM)[name] if last is None else last
                with pe.Fori(first // SLOTS, last // SLOTS) as i:
                    for j in range(SLOTS):
                        pe.wait_ge(slot_ready[j], 16 * (FIRST[name] // SLOTS) + 16 + i * 16)
                        pe.wait_ge(freed, base + i * SLOTS + j - 3)
                        for k, w in enumerate(tiles(j)):
                            if j == 0 and h is not None:
                                pe.wait_ge(h_ready, KT * h + k + 1)
                            ins = mm(PS[:, j, :], w, rhs[:, k, :], k == 0, k == KT - 1)
                        ins.then_inc(blocks_done, 1)

            def norm(n):
                for k in range(KT):
                    pe.wait_ge(sq_ready, KT * n + k + 1)
                    mm(PS[:, 7, :], ones, sq[:, k % 2, :], k == 0, k == KT - 1).then_inc(sq_used, 1)

            def columns(src, blk, g):
                for q in range(4):
                    ins = mm(PS[:, 6, 48 * blk + 4 * g + q:48 * blk + 4 * g + q + 1], src[:, g, q * P:(q + 1) * P], ones[:, 0:1])
                ins.then_inc(modcol_done, 1)

            pe.wait_ge(inputs_loaded, 32)
            norm(0)
            for g in range(12):
                pe.wait_ge(blocks_done, SLOTS * (g + 1))
                columns(acc, 0, g)
            pe.wait_ge(rest_loaded, 48)
            for c in range(NC):
                for k in range(KT):
                    if c == 0:
                        pe.wait_ge(h_ready, k + 1)
                    ins = mm(PS[:, c, :NROW], hT[:, k, c * P:(c + 1) * P], roww[:, k, :], k == 0, k == KT - 1)
                ins.then_inc(rows_done, 1)
            pe.wait_ge(row_evac, 2 * NC)
            gemm("w_in", hT, row_evac, 2 * NC, 0, 4)
            gemm("w_in", hT, conv_ready, 0, 4, 16)
            gemm("w_in", hT, zq_ready, -12, 16, 24)
            pe.wait_ge(g_ready, 1)
            mm(PS[:, 4, 0:16], cst("upper"), gsm[:, 5, :])
            mm(PS[:, 4, 16:32], ones, gsm[:, 5, :]).then_inc(gc_done, 1)
            pe.wait_ge(e3_in, 1)

            def head_norm(n, width=S):
                pe.wait_ge(hs_ready, n + 1)
                if n >= 4:
                    pe.wait_ge(hs_std, n - 3)
                mm(PS[:, 4 + n % 4, :width], ones, sq[:, n % 2, :width]).then_inc(hs_used, 1)

            for t in range(MANY):
                pe.wait_ge(hm_ready, t + 1)
                mm(PS[0:MANY, 5, :], cst("strip")[:, MANY - 1 - t:2 * MANY - 1 - t], sq[:, t % 2, :], t == 0, t == MANY - 1
                   ).then_inc(hm_used, 1)
            pe.wait_ge(hm_recip, 1)
            for t in range(MANY):
                if t >= 4:
                    pe.wait_ge(hm_normed, t - 3)
                mm(PS[:, t % 4, :], select[0:MANY, t, :], rs[0:MANY, 0, :]).then_inc(hm_bc, 1)
            pe.wait_ge(hm_normed, MANY)
            pe.wait_ge(ug_ready, 2)
            for h in range(NH):
                b = 4 * (h % 2)
                if h >= 2:
                    pe.wait_ge(prep_done, h - 1)
                    pe.wait_ge(eg_ready, h - 1)
                mm(PS[:, b, :], ones, Ug[:, h, :, :].rearrange("p c n -> p (c n)"))
                mm(PS[:, b + 1, :], ones, Ib[:, h, :, :].rearrange("p c n -> p (c n)"))
                for c in range(NC):
                    t = slice(c * P, (c + 1) * P)
                    mm(PS[:, b + 2, t], qkv[:, 4 + h, t], qkv[:, 4 + h, t])
                for c in range(NC):
                    t = slice(c * P, (c + 1) * P)
                    ins = mm(PS[:, b + 3, t], qkv[:, 4 + h, t], qkv[:, h, t])
                ins.then_inc(prep_ps, 1)
            pe.wait_ge(prep_done, NH)
            for n in range(8):
                if n >= 2:
                    pe.wait_ge(kv_done, n - 1)
                for c in range(NC):
                    t = slice(c * P, (c + 1) * P)
                    ins = nc.tensor.transpose(PS[:, n % 2, t], qkv[:, 4 + n, t], ident)
                ins.then_inc(tr_ready, 1)
            pe.wait_ge(kv_done, 8)
            def second(i, h):
                pe.wait_ge(y_ready, i * NH + h + 1)
                pe.wait_ge(tt_ready, i * NH + h + 3)
                for c in range(NC):
                    mm(PS[:, 2 + h % 2, c * P:(c + 1) * P], TT[:, h, c, :], Y[:, h, c, :])
                for c in range(NC):
                    ins = mm(PS[:, 4 + h % 2, c * P:(c + 1) * P], Y[:, h, c, :], TT[:, h, c, :])
                ins.then_inc(pq_done, 1)

            with pe.Fori(0, LEVELS) as i:
                for h in range(NH):
                    pe.wait_ge(am_ready, i * NH + h + 1)
                    pe.wait_ge(tt_ready, i * NH + h + 1)
                    for c in range(NC):
                        ins = mm(PS[:, h % 2, c * P:(c + 1) * P], Am[:, h, c, :], Tm[:, h, c, :])
                    ins.then_inc(y_done, 1)
                    if h:
                        second(i, h - 1)
                second(i, NH - 1)
            pe.wait_ge(tt_ready, NH * LEVELS + NH)
            for h in range(NH):
                b = 2 * (h % 2)
                if h >= 2:
                    pe.wait_ge(u_ready, h - 1)
                    pe.wait_ge(w_ready, h - 1)
                for c in range(NC):
                    mm(PS[:, b, c * P:(c + 1) * P], TT[:, h, c, :], vb[:, h, c, :])
                for c in range(NC):
                    ins = mm(PS[:, b + 1, c * P:(c + 1) * P], kbg[:, h, c, :], TT[:, h, c, :])
                ins.then_inc(uw_done, 1)
            pe.wait_ge(u_ready, NH)
            pe.wait_ge(w_ready, NH)
            for c in range(NC):
                t = slice(c * P, (c + 1) * P)
                pe.wait_ge(state_ready, NH * c + 1)
                for h in range(NH):
                    hh = slice(h * P, (h + 1) * P)
                    ins = mm(PS[:, 0, hh], wT[:, h, c, :], Sst[:, h, :])
                ins.then_inc(ws_done, 1)
                pe.wait_ge(vnew_ready, c + 1)
                if c >= 2:
                    pe.wait_ge(o_ready, c - 1)
                for h in range(NH):
                    hh = slice(h * P, (h + 1) * P)
                    mm(PS[:, 1 + c % 2, hh], Sst[:, h, :], qdT[:, h, t], True, False)
                    ins = mm(PS[:, 1 + c % 2, hh], vn[:, h, :], attnT[:, h, c, :], False, True)
                ins.then_inc(o_done, 1)
                for h in range(NH):
                    ins = mm(PS[:, 3, h * P:(h + 1) * P], kd[:, h, c, :], vn[:, h, :])
                ins.then_inc(s_done, 1)
            for h in range(NH):
                head_norm(h)
            pe.wait_ge(kcp_ready, 2)
            for z in range(2):
                for b in range(4):
                    j = b
                    pe.wait_ge(slot_ready[j], 16 * (FIRST["cmp"] // SLOTS + z + 1))
                    for k in range(KT):
                        n = b * KT + k
                        ins = mm(PS[:, z, :NCMP], ring[:, j, k * P:(k + 1) * P], kcp[:, z, n, :], n == 0, n == CMP_L - 1)
                    ins.then_inc(blocks_done, 1)
            pe.wait_ge(hid_ready, 2)
            pe.wait_ge(og_ready, NH)
            mm(PS[:, 2, :NCMP], mat("w2k"), hid[:, 0, :])
            mm(PS[:NCMP, 3, :HD], hid[:, 1, :], mat("w2v")).then_inc(kc_done, 1)
            head_norm(4, NCMP)
            pe.wait_ge(hs_normed, 5)
            pe.wait_ge(vc_ready, 1)
            def scores(n):
                c, h = divmod(n, NH)
                if n >= 1:
                    pe.wait_ge(sc_ready, n)
                if n >= 2:
                    pe.wait_ge(p_ready, 3 * (n - 1))
                q = mix[:, 4 + h, c * P:(c + 1) * P]
                N = (c + 1) * P
                mm(PS[:, 2 * (n % 2), :N], q, kswn[:, 0, :N])
                mm(PS[:, 2 * (n % 2) + 1, :N], q, kswn[:, 1, :N])
                mm(PS[:, 4, :NCMP], q, kct[:, :NCMP]).then_inc(sc_done, 1)

            scores(0)
            scores(1)
            for n in range(NC * NH):
                c, h = divmod(n, NH)
                pe.wait_ge(pn_ready, 2 * (n + 1))
                if n >= 1:
                    pe.wait_ge(pt_act, 2 * n)
                    pe.wait_ge(pt_vec, n)
                    pe.wait_ge(att_ready, n)
                for k in range(c + 1):
                    nc.tensor.transpose(PS[:, 6, k * P:(k + 1) * P], Pm[:, n % 2, 0, k * P:(k + 1) * P], ident)
                for k in range(c + 1):
                    nc.tensor.transpose(PS[:, 7, k * P:(k + 1) * P], Pm[:, n % 2, 1, k * P:(k + 1) * P], ident)
                nc.tensor.transpose(PS[:NCMP, 5, P:2 * P], Pc[:, n % 2, :NCMP], ident
                                    ).then_inc(pt_done, 1)
                if n + 2 < NC * NH:
                    scores(n + 2)
                pe.wait_ge(pt_act, 2 * (n + 1))
                pe.wait_ge(pt_vec, n + 1)
                o = PS[:, 5, 2 * P:3 * P]
                for k in range(c + 1):
                    for z in range(2):
                        mm(o, vrow[:, k, z, :], PT[:, n % 2, 4 * z + k, :], k + z == 0, False)
                mm(o, vcr[:NCMP, :], PT[:NCMP, n % 2, 8, :], False, True).then_inc(av_done, 1)
            pe.wait_ge(att_ready, NC * NH)
            gemm("w_out", mix, att_ready, NC * NH, 0, 4)
            gemm("w_out", mix, x1_ready, 0, 4, 8)
            norm(1)
            gemm("up", hT, x1_ready, 8, 0, 4, h=1)
            gemm("up", hT, fy_ready, 0, 4)
            pe.wait_ge(ff_ready, FT)
            for m in range(KT):
                if m == 1:
                    pe.wait_ge(ada_2_used, 48)
                    for g in range(12):
                        columns(acc_2, 1, g)
                if m >= 4:
                    pe.wait_ge(x2_ready, m - 3)
                for u in range(2):
                    q = 2 * m + u
                    pe.wait_ge(slot_ready[q % SLOTS], 16 * ((FIRST["down"] + q) // SLOTS + 1))
                    for k in range(FT // 2):
                        kk = u * (FT // 2) + k
                        ins = mm(PS[:, m % 4, :], ring[:, q % SLOTS, k * P:(k + 1) * P], gT[:, kk, :], kk == 0, kk == FT - 1)
                    ins.then_inc(blocks_done, 1)
            norm(2)
            gemm("w_in_2", hT, x2_ready, 8, 0, 4, h=2)
            gemm("w_in_2", hT, sg_ready, 0, 4)
            for g in range(4):
                pe.wait_ge(pm_ready, g + 1)
                pe.wait_ge(sg_ready, 28)
                mm(PS[:, g, :], mat("poolw")[:, g * P:(g + 1) * P], mx4[:, g, :]).then_inc(pool_done, 1)
            pe.wait_ge(ln_in, 1)
            for g in range(4):
                ins = mm(PS[:, 4, :], ones, yc[:, g, :], g == 0, g == 3)
            ins.then_inc(ln_sum1, 1)
            for g in range(4):
                pe.wait_ge(ln_sq, g + 1)
                mm(PS[:, 5, :], ones, sq[:, g % 2, :], g == 0, g == 3).then_inc(ln_sum2, 1)
            pe.wait_ge(yc_ready, 4)
            pe.wait_ge(pscaled, 4)
            for m in range(KT):
                j, b = m % SLOTS, 2 * (m % 2)
                pe.wait_ge(slot_ready[j], 16 * ((FIRST["branch"] + m) // SLOTS + 1))
                if m >= 2:
                    pe.wait_ge(m_half, m - 1)
                for k in range(4):
                    mm(PS[:, b, :], ring[:, j, k * P:(k + 1) * P], pmT[:, k, :], k == 0, k == 3)
                for k in range(4):
                    ins = mm(PS[:, b + 1, :], ring[:, j, (4 + k) * P:(5 + k) * P], yc[:, k, :], k == 0, k == 3)
                ins.then_inc(blocks_done, 1)
            pe.wait_ge(merged, 8)
            gemm("w_out_2", mg, merged, 8, 0, 4)
            gemm("w_out_2", mg, x3_ready, 0, 4)
            norm(3)
            gemm("query", hT, x3_ready, 8, 0, 4, h=3)
            pe.wait_ge(q_ready, 4)
            for m in range(4):
                ins = mm(PS[:, 5, m * P:(m + 1) * P], qT[:, m, 0:P], mat("keys1") if m % 2 == 0 else mat("keys2"))
            ins.then_inc(sc2_done, 1)
            gemm("query", hT, q_ready, 0, 4)
            pe.wait_ge(q_ready, 16)
            for c in range(NC):
                for g in range(1 if c == 0 else 0, 4):
                    if c:
                        pe.wait_ge(sc2_ready, 4 * (c - 1) + g + 1)
                    for u in range(4):
                        m = 4 * g + u
                        ins = mm(PS[:, g, u * P:(u + 1) * P], qT[:, m, c * P:(c + 1) * P],
                                 mat("keys1") if m % 2 == 0 else mat("keys2"))
                    ins.then_inc(sc2_done, 1)
            for n in range(2 * NC):
                c, half = divmod(n, 2)
                if n >= 2:
                    pe.wait_ge(hr_ready, n - 1)
                for k in range(4):
                    ins = nc.tensor.transpose(PS[:, 4 + n % 2, k * P:(k + 1) * P],
                                              hT[:, 4 * half + k, c * P:(c + 1) * P], ident)
                ins.then_inc(hr_done, 1)
            def step(c, h, start=False, stop=False):
                for q in range(SB):
                    pe.wait_ge(diag_ready, (c * HEADS) * SB + h * SB + q + 1)
                    for k in range(BATCH):
                        r = (q * BATCH + k) % RING
                        for v in range(2):
                            ins = mm(PS[:, 4 * (c % 2) + v, :], diag[:, q % NB, k, :],
                                     ring_e[:, r, D + v * S:D + (v + 1) * S],
                                     start and q + k == 0, stop and q == SB - 1 and k == BATCH - 1)
                    ins.then_inc(rows_used, 1)

            def turn_tile(c):
                pe.wait_ge(prow_ready, 2 * (c + 1))
                if c:
                    pe.wait_ge(x4_ready, KT * c)
                for v in range(2):
                    for k in range(4):
                        ins = nc.tensor.transpose(PS[:, 2 + v, k * P:(k + 1) * P], prow[:, (4 * v + k) * P:(4 * v + k + 1) * P], ident)
                    ins.then_inc(pt2_done, 1)

            def sum_squares(c):
                pe.wait_ge(fin_sq, c + 1)
                if c:
                    pe.wait_ge(fin_std, c)
                for k in range(KT):
                    ins = mm(PS[:, 7, 0:P], ones, fsq[:, k, :], k == 0, k == KT - 1)
                ins.then_inc(fin_sum, 1)

            for c in range(NC):
                step(c, 0, start=True)
                if c:
                    turn_tile(c - 1)
                step(c, 1)
                with pe.Fori(2, HEADS - 1) as h:
                    step(c, h)
                step(c, HEADS - 1, stop=True)
                if c:
                    sum_squares(c - 1)
            turn_tile(NC - 1)
            sum_squares(NC - 1)

        @block.scalar
        def _(act):
            n = Count()
            A = nc.scalar.activation

            act.wait_ge(params_loaded, 16)
            A(silc[:, 0, :], par("c", 0, KT), ACT.Silu).then_inc(silu_c_ready, 1)
            act.wait_ge(silu_c_ready, n(silu_c_ready))
            A(silc[:, 1, :], par("c_2", 0, KT), ACT.Silu).then_inc(silu_c_ready, 1)
            act.wait_ge(silu_c_ready, n(silu_c_ready))
            def norm(z, col, shift, final=None, base=0):
                for k in range(KT):
                    if KT * z + k >= 2:
                        act.wait_ge(sq_used, KT * z + k - 1)
                    if final is not None:
                        act.wait_ge(final, base + k + 1)
                    A(sq[:, k % 2, :], xT[:, k, :], ACT.Square).then_inc(sq_ready, 1)
                    act.wait_ge(sq_ready, n(sq_ready))
                act.wait_ge(sq_used, KT * (z + 1))
                A(rs[:, 0, :], PS[:, 7, :], ACT.Sqrt, bias=eps, scale=1.0 / D).then_inc(std_ready, 1)
                act.wait_ge(std_ready, n(std_ready))
                if z in (0, 2):
                    act.wait_ge(mod_ready, z // 2 + 1)
                for k in range(KT):
                    act.wait_ge(normed, KT * z + k + 1)
                    A(hT[:, k, :], hT[:, k, :], ACT.Identity, bias=shift(k), scale=eff[:, col, k:k + 1]).then_inc(h_ready, 1)
                    act.wait_ge(h_ready, n(h_ready))

            act.wait_ge(inputs_loaded, 32)
            norm(0, 0, lambda k: mod[:, 0, k:k + 1])
            for c in range(NC):
                act.wait_ge(rows_done, c + 1)
                A(vrow[:, c, :, :].rearrange("p z d -> p (z d)"), PS[:, c, :2 * HD], ACT.Copy).then_inc(row_evac, 1)
                act.wait_ge(row_evac, n(row_evac))
                A(small[:, c, :], PS[:, c, 2 * HD:NROW], ACT.Copy).then_inc(row_evac, 1)
                act.wait_ge(row_evac, n(row_evac))
            with act.Fori(0, 6) as i:
                n.enter(i, (qkv_ready, 2))
                for u in range(2):
                    act.wait_ge(conv_ready, i * 2 + u + 1)
                    A(qkv[:, bass.ds(i * 2 + u, 1), :].rearrange("p o n -> p (o n)"), cv[:, u, :], ACT.Silu).then_inc(qkv_ready, 1)
                    act.wait_ge(qkv_ready, n(qkv_ready))
                n.leave(6)
            for m in range(12, 24):
                act.wait_ge(blocks_done, FIRST["w_in"] + m + 1)
                dst = mix[:, m - 12, :] if m < 20 else (kcvc[:, m - 20, :] if m < 22 else kswn[:, m - 22, :])
                A(dst, PS[:, m % 4, :], ACT.Silu if m < 16 else ACT.Copy).then_inc(zq_ready, 1)
                act.wait_ge(zq_ready, n(zq_ready))
            A(sgm, small[:, :, NH:], ACT.Sigmoid).then_inc(gate_sg, 1)
            act.wait_ge(gate_sg, n(gate_sg))
            act.wait_ge(gate_nz, 1)
            A(gsm[:, 2, :], gsm[:, 1, :], ACT.Exp).then_inc(gate_e, 1)
            act.wait_ge(gate_e, n(gate_e))
            A(gsm[:, 3, :], gsm[:, 2, :], ACT.Ln, bias=one).then_inc(gate_ln, 1)
            act.wait_ge(gate_ln, n(gate_ln))
            A(gsm[:, 4, :], par("a_log", 0, 16), ACT.Exp).then_inc(gate_ea, 1)
            act.wait_ge(gate_ea, n(gate_ea))
            act.wait_ge(e3_in, 1)
            A(e3, g3, ACT.Exp).then_inc(e3_ready, 1)
            act.wait_ge(e3_ready, n(e3_ready))

            def head_norm(t, src, scale, width=S):
                if t >= 2:
                    act.wait_ge(hs_used, t - 1)
                A(sq[:, t % 2, :width], src, ACT.Square).then_inc(hs_ready, 1)
                act.wait_ge(hs_ready, n(hs_ready))
                act.wait_ge(hs_used, t + 1)
                if t >= 2:
                    act.wait_ge(hs_normed, t - 1)
                A(rs[:, t % 2, :width], PS[:, 4 + t % 4, :width], ACT.Sqrt, bias=eps, scale=scale).then_inc(hs_std, 1)
                act.wait_ge(hs_std, n(hs_std))

            for t in range(MANY):
                src = qkv[:, t, :] if t < 8 else (mix[:, t - 4, :] if t < 12 else kswn[:, t - 12, :])
                if t >= 2:
                    act.wait_ge(hm_used, t - 1)
                A(sq[:, t % 2, :], src, ACT.Square).then_inc(hm_ready, 1)
            act.wait_ge(hm_used, MANY)
            A(rs[0:MANY, 0, :], PS[0:MANY, 5, :], ACT.Sqrt, bias=eps[0:MANY], scale=cst("hscale")[0:MANY]).then_inc(hm_std, 1)
            for h in range(NH):
                act.wait_ge(prep_ps, h + 1)
                act.wait_ge(dec_in, h + 1)
                A(eg, PS[:, 4 * (h % 2), :], ACT.Exp).then_inc(eg_ready, 1)
                act.wait_ge(eg_ready, n(eg_ready))
                A(t1[:, h % 2, :], t1[:, h % 2, :], ACT.Exp).then_inc(dec_exp, 1)
                act.wait_ge(dec_exp, n(dec_exp))
            with act.Fori(0, LEVELS) as i:
                n.enter(i, (y_ready, NH))
                for h in range(NH):
                    act.wait_ge(y_done, i * NH + h + 1)
                    A(Y[:, h, :, :].rearrange("p c n -> p (c n)"), PS[:, h % 2, :], ACT.Copy).then_inc(y_ready, 1)
                    act.wait_ge(y_ready, n(y_ready))
                n.leave(LEVELS)
            for h in range(NH):
                act.wait_ge(uw_done, h + 1)
                A(Um[:, h, :, :].rearrange("p c n -> p (c n)"), PS[:, 2 * (h % 2), :], ACT.Copy).then_inc(u_ready, 1)
                act.wait_ge(u_ready, n(u_ready))
            for c in range(NC):
                act.wait_ge(o_done, c + 1)
                A(oT[:, :, c * P:(c + 1) * P], PS[:, 1 + c % 2, :].rearrange("p (h n) -> p h n", h=NH), ACT.Copy).then_inc(o_ready, 1)
                act.wait_ge(o_ready, n(o_ready))
            for h in range(NH):
                head_norm(h, oT[:, h, :], 1.0 / HD)
            for z in range(2):
                act.wait_ge(blocks_done, FIRST["cmp"] + 4 * (z + 1))
                A(hid[:, z, :], PS[:, z, :NCMP], ACT.Silu).then_inc(hid_ready, 1)
                act.wait_ge(hid_ready, n(hid_ready))
            act.wait_ge(kc_done, 1)
            A(kct[:, :NCMP], PS[:, 2, :NCMP], ACT.Copy).then_inc(kc_ready, 1)
            act.wait_ge(kc_ready, n(kc_ready))
            A(vcr[:NCMP, :], PS[:NCMP, 3, :HD], ACT.Copy).then_inc(vc_ready, 1)
            act.wait_ge(vc_ready, n(vc_ready))
            head_norm(4, kct[:, :NCMP], 1.0 / HD, NCMP)
            def exps(t):
                c, h = divmod(t, NH)
                N = (c + 1) * P
                act.wait_ge(negm_ready, t + 1)
                m = mx[:, t % 2, :]
                A(Pm[:, t % 2, 0, :N], PS[:, 2 * (t % 2), :N], ACT.Exp, bias=m[:, 4:5], scale=SCALE, accum_out=m[:, 7:8]).then_inc(p_ready, 1)
                A(Pm[:, t % 2, 1, :N], PS[:, 2 * (t % 2) + 1, :N], ACT.Exp, bias=m[:, 5:6], scale=SCALE, accum_out=m[:, 8:9]).then_inc(p_ready, 1)
                act.wait_ge(sc_sub, t + 1)
                A(Pc[:, t % 2, :NCMP], sc[:, t % 2, :NCMP], ACT.Exp, scale=SCALE, accum_out=m[:, 6:7]).then_inc(p_ready, 1)

            exps(0)
            for t in range(NC * NH):
                c, h = divmod(t, NH)
                N = (c + 1) * P
                if t + 1 < NC * NH:
                    exps(t + 1)
                act.wait_ge(pt_done, t + 1)
                if t >= 2:
                    act.wait_ge(av_done, t - 1)
                A(PT[:, t % 2, 0:c + 1, :], PS[:, 6, :N].rearrange("p (k q) -> p k q", q=P), ACT.Copy).then_inc(pt_act, 1)
                A(PT[:NCMP, t % 2, 8, :], PS[:NCMP, 5, P:2 * P], ACT.Copy).then_inc(pt_act, 1)
                act.wait_ge(av_done, t + 1)
                A(mix[:, 4 + h, c * P:(c + 1) * P], PS[:, 5, 2 * P:3 * P], ACT.Copy).then_inc(att_ready, 1)
            norm(1, 1, lambda k: mod[:, 0, 24 + k:25 + k], x1_ready, 0)
            with act.Fori(0, FT // 2) as i:
                n.enter(i, (sa_ready, 2))
                for u in range(2):
                    act.wait_ge(fy_ready, i * 4 + 2 * u + 1)
                    A(sa[:, u, :], y0[:, u, :], ACT.Silu).then_inc(sa_ready, 1)
                    act.wait_ge(sa_ready, n(sa_ready))
                n.leave(FT // 2)
            norm(2, 2, lambda k: mod[:, 1, k:k + 1], x2_ready, 0)
            for m in range(28):
                act.wait_ge(blocks_done, FIRST["w_in_2"] + m + 1)
                src = PS[:, m % 4, :]
                b = par("b_in", m)
                if m < 4:
                    A(pT[:, m, 16:], src, ACT.Identity, bias=b).then_inc(sg_ready, 1)
                    act.wait_ge(sg_ready, n(sg_ready))
                elif m < 12:
                    t = (m - 4) // 2
                    if m % 2 == 0 and t >= 2:
                        act.wait_ge(glu_ready, t - 1)
                    if m % 2 == 0:
                        A(a1[:, t % 2, :], src, ACT.Identity, bias=b).then_inc(sg_ready, 1)
                        act.wait_ge(sg_ready, n(sg_ready))
                    else:
                        A(a2[:, t % 2, :], src, ACT.Sigmoid, bias=b).then_inc(sg_ready, 1)
                        act.wait_ge(sg_ready, n(sg_ready))
                else:
                    A(sgT[:, m - 12, :], src, ACT.Sigmoid, bias=b).then_inc(sg_ready, 1)
                    act.wait_ge(sg_ready, n(sg_ready))
            for g in range(4):
                act.wait_ge(pool_done, g + 1)
                A(pmT[:, g, :], PS[:, g, :], ACT.Copy, scale=par("pscale", g)).then_inc(pscaled, 1)
                act.wait_ge(pscaled, n(pscaled))
            act.wait_ge(ln_sum1, 1)
            A(lnm, PS[:, 4, :], ACT.Copy, scale=1.0 / S).then_inc(ln_mu, 1)
            act.wait_ge(ln_mu, n(ln_mu))
            for g in range(4):
                act.wait_ge(ln_y, g + 1)
                if g >= 2:
                    act.wait_ge(ln_sum2, g - 1)
                A(sq[:, g % 2, :], yc[:, g, :], ACT.Square).then_inc(ln_sq, 1)
                act.wait_ge(ln_sq, n(ln_sq))
            act.wait_ge(ln_sum2, 4)
            A(rs[:, 0, :], PS[:, 5, :], ACT.Sqrt, bias=eps, scale=1.0 / S).then_inc(ln_std, 1)
            act.wait_ge(ln_std, n(ln_std))
            for g in range(4):
                act.wait_ge(ln_y, 4 + g + 1)
                A(yc[:, g, :], yc[:, g, :], ACT.Silu).then_inc(yc_ready, 1)
                act.wait_ge(yc_ready, n(yc_ready))
            norm(3, 3, lambda k: mod[:, 1, 24 + k:25 + k], x3_ready, 0)
            def exp_gates(par_, value):
                act.wait_ge(sm_in, value)
                A(gcur[:, par_, :], gcur[:, par_, :], ACT.Exp, accum_out=gsum[:, par_, 0:1]).then_inc(sm_exp, 1)

            for m in range(16):
                act.wait_ge(blocks_done, FIRST["query"] + m + 1)
                A(qT[:, m, :], PS[:, m % 4, :], ACT.Copy).then_inc(q_ready, 1)
                act.wait_ge(q_ready, n(q_ready))
                if m == 3:
                    act.wait_ge(sc2_done, 1)
                    A(sS[:, 0:2, :].rearrange("p u n -> p (u n)"), PS[:, 5, :], ACT.Copy).then_inc(sc2_ready, 1)
                if m == 7:
                    exp_gates(0, 1)
                if m == 11:
                    exp_gates(1, 2)
            for c in range(NC):
                for g in range(1 if c == 0 else 0, 4):
                    act.wait_ge(sc2_done, 4 * c + g + 1)
                    A(sS[:, c * HEADS + 2 * g:c * HEADS + 2 * g + 2, :].rearrange("p u n -> p (u n)"), PS[:, g, :], ACT.Copy).then_inc(sc2_ready, 1)
            def step(s_, par_):
                act.wait_ge(gate_ready, s_ + 1)
                for q in range(SB):
                    b = q % NB
                    act.wait_ge(dots_ready, s_ * TOPK + BATCH * (q + 1))
                    A(wts[:, b, :], dots[:, b, :], ACT.Gelu_apprx_tanh).then_inc(gelu_ready, 1)
                    act.wait_ge(gelu_ready, n(gelu_ready))
                    for k in range(BATCH):
                        A(wts[:, b, k:k + 1], wts[:, b, k:k + 1], ACT.Copy, scale=gcur[:, par_, q * BATCH + k:q * BATCH + k + 1]
                          ).then_inc(w_ready2, 1)
                    act.wait_ge(w_ready2, n(w_ready2) + BATCH - 1)
                    n(w_ready2)
                    A(diag[:, b, 0, :], ident, ACT.Copy, scale=wts[:, b, 0:1]).then_inc(act_step, 1)
                    A(diag[:, b, 1, :], ident, ACT.Copy, scale=wts[:, b, 1:2]).then_inc(diag_ready, 1)

            def square_tile(c):
                act.wait_ge(x4_ready, KT * (c + 1))
                A(fsq, xT[:, :, c * P:(c + 1) * P], ACT.Square).then_inc(fin_sq, 1)

            def deviation(c):
                act.wait_ge(fin_sum, c + 1)
                A(rs[:, c % 2, 0:P], PS[:, 7, 0:P], ACT.Sqrt, bias=eps, scale=1.0 / D).then_inc(fin_std, 1)

            for c in range(NC):
                def pair(i, more, first_pair=False):
                    for u in range(2):
                        step(i * 2 + (c * HEADS + u), u)
                        if first_pair and u == 0:
                            if c > 1:
                                act.wait_ge(pt2_done, 2 * (c - 1))
                            act.wait_ge(rows_used, SB * HEADS * c)
                            for v in range(2):
                                A(prow[:, v * S:(v + 1) * S], PS[:, 4 * ((c - 1) % 2) + v, :], ACT.Copy).then_inc(prow_ready, 1)
                            if c > 1:
                                deviation(c - 2)
                        if more:
                            exp_gates(u, i * 2 + (c * HEADS + u + 3))
                pair(0, True, first_pair=c > 0)
                end = c == NC - 1
                with act.Fori(1, 3 if end else 4) as i:
                    n.enter(i - 1, (gelu_ready, 2 * SB), (w_ready2, 2 * TOPK))
                    pair(i, True)
                    n.leave(2 if end else 3)
                if end:
                    pair(3, False)
                if c:
                    square_tile(c - 1)
            act.wait_ge(rows_used, SB * HEADS * NC)
            act.wait_ge(pt2_done, 2 * (NC - 1))
            for v in range(2):
                A(prow[:, v * S:(v + 1) * S], PS[:, 4 * ((NC - 1) % 2) + v, :], ACT.Copy).then_inc(prow_ready, 1)
            deviation(NC - 2)
            square_tile(NC - 1)
            deviation(NC - 1)

        @block.vector
        def _(dve):
            n = Count()
            V = nc.vector

            def tt(o, x, y, op):
                return V.tensor_tensor(out=o, in0=x, in1=y, op=op)

            def ts(o, x, s1, s2, op0, op1):
                return V.tensor_scalar(o, x, s1, s2, op0, op1)

            def stt(o, x, s_, y, op0, op1):
                return V.scalar_tensor_tensor(out=o, in0=x, scalar=s_, in1=y, op0=op0, op1=op1)

            def copy(o, x):
                return V.tensor_copy(o, x)

            def last(v, many):
                return v.unsqueeze(len(v.shape)).to_broadcast(list(v.shape) + [many])

            def mid(v, *many):
                for q in many:
                    v = v.unsqueeze(1)
                return v.to_broadcast([v.shape[0], *many, v.shape[-1]])

            def flat(v):
                return v.rearrange("p c n -> p (c n)")


            MUL, ADD, SUB, MAX, MIN = ALU.mult, ALU.add, ALU.subtract, ALU.max, ALU.min
            def modulation(blk):
                dve.wait_ge(modcol_done, 12 * (blk + 1))
                tt(mod[:, blk, :], PS[:, 6, 48 * blk:48 * blk + 48], par("ada_b" if blk == 0 else "ada_b_2", 0, 48), ADD).then_inc(vec_step, 1)
                dve.wait_ge(vec_step, n(vec_step))
                for u, g in enumerate(("norm1", "norm2") if blk == 0 else ("norm1_2", "norm2_2")):
                    stt(eff[:, 2 * blk + u, :], mod[:, blk, 8 + 24 * u:16 + 24 * u], 1.0, par(g, 0, KT), ADD, MUL).then_inc(mod_ready if u else vec_step, 1)
                    dve.wait_ge(mod_ready if u else vec_step, n(mod_ready if u else vec_step))

            def matvec(blk, g, weights, landed, used, dst):
                for k in range(KT):
                    j, u = divmod(k, 2)
                    if u == 0:
                        dve.wait_ge(landed[j], g * 16 + 16)
                    w = weights[:, j, u * S:(u + 1) * S]
                    c_ = silc[:, blk, k:k + 1]
                    if k == 0:
                        ts(dst, w, c_, None, MUL, ALU.bypass).then_inc(vec_step, 1)
                    else:
                        stt(dst, w, c_, dst, MUL, ADD).then_inc(used if u else vec_step, 1)
                    dve.wait_ge(used if u else vec_step, n(used if u else vec_step))

            def norm(t):
                dve.wait_ge(std_ready, t + 1)
                V.reciprocal(rs[:, 0, :], rs[:, 0, :]).then_inc(vec_step, 1)
                dve.wait_ge(vec_step, n(vec_step))
                for k in range(KT):
                    tt(hT[:, k, :], xT[:, k, :], rs[:, 0, :], MUL).then_inc(normed, 1)
                    dve.wait_ge(normed, n(normed))

            dve.wait_ge(inputs_loaded, 32)
            norm(0)
            dve.wait_ge(silu_c_ready, 2)
            matvec(0, 0, ring, slot_ready, blocks_done, acc[:, 0, :])
            with dve.Fori(1, 12) as i:
                n.enter(i - 1, (blocks_done, SLOTS), (vec_step, SLOTS))
                matvec(0, i, ring, slot_ready, blocks_done, acc[:, bass.ds(i, 1), :].rearrange("p o n -> p (o n)"))
                n.leave(11)
            modulation(0)
            def conv4(i, fresh):
                for j in range(SLOTS):
                    dve.wait_ge(blocks_done, FIRST["w_in"] + i * SLOTS + j + 1)
                    if not fresh or j >= 2:
                        dve.wait_ge(qkv_ready, i * SLOTS + j - 1)

                    def tap(t):
                        return param[:, bass.ds(i * 16 + (PARAM["gconv"][0] + 4 * j + t), 1)]
                    o = cv[:, j % 2, :]
                    ts(o, PS[:, j, :], tap(3), None, MUL, ALU.bypass).then_inc(vec_step, 1)
                    dve.wait_ge(vec_step, n(vec_step))
                    for t in (1, 2, 3):
                        stt(o[:, t:], PS[:, j, :S - t], tap(3 - t), o[:, t:], MUL, ADD).then_inc(conv_ready if t == 3 else vec_step, 1)
                        dve.wait_ge(conv_ready if t == 3 else vec_step, n(conv_ready if t == 3 else vec_step))

            conv4(0, True)
            with dve.Fori(1, 3) as i:
                n.enter(i - 1, (conv_ready, SLOTS), (vec_step, 3 * SLOTS))
                conv4(i, False)
                n.leave(2)
            dve.wait_ge(zq_ready, 12)
            dve.wait_ge(qkv_ready, 12)
            dve.wait_ge(row_evac, 2 * NC)
            tt(gsm[:, 0, :].rearrange("p (c h) -> p c h", h=NH), small[:, :, 0:NH], par("dt", 0, 16).rearrange("p (c h) -> p c h", h=NH), ADD).then_inc(vec_step, 1)
            dve.wait_ge(vec_step, n(vec_step))
            stt(gsm[:, 1, :], gsm[:, 0, :], -1.0, gsm[:, 0, :], MUL, MIN).then_inc(gate_nz, 1)
            dve.wait_ge(gate_nz, n(gate_nz))
            dve.wait_ge(gate_ln, 1)
            stt(gsm[:, 6, :], gsm[:, 0, :], 0.0, gsm[:, 3, :], MAX, ADD).then_inc(vec_step, 1)
            dve.wait_ge(vec_step, n(vec_step))
            dve.wait_ge(gate_ea, 1)
            stt(gsm[:, 5, :], gsm[:, 6, :], -1.0, gsm[:, 4, :], MUL, MUL).then_inc(g_ready, 1)
            dve.wait_ge(g_ready, n(g_ready))
            dve.wait_ge(gc_done, 1)
            copy(gcl.rearrange("p z n -> p (z n)"), PS[:, 4, 0:32]).then_inc(vec_step, 1)
            dve.wait_ge(vec_step, n(vec_step))
            tt(g3[:, 0, :], gcl[:, 1, :], gcl[:, 0, :], SUB).then_inc(vec_step, 1)
            dve.wait_ge(vec_step, n(vec_step))
            copy(g3[:, 1:3, :].rearrange("p z n -> p (z n)"), gcl.rearrange("p z n -> p (z n)")).then_inc(e3_in, 1)
            dve.wait_ge(e3_in, n(e3_in))
            dve.wait_ge(e3_ready, 1)
            dve.wait_ge(gate_sg, 1)
            beta = sgm[:, :, 0:NH]
            tt(kb.rearrange("p (c h) -> p c h", h=NH), e3[:, 1, :].rearrange("p (c h) -> p c h", h=NH), beta, MUL).then_inc(vec_step, 1)
            dve.wait_ge(vec_step, n(vec_step))

            def head_norm(t, dst, gain, width=S):
                dve.wait_ge(hs_std, t + 1)
                r = rs[:, t % 2, :width]
                V.reciprocal(r, r).then_inc(vec_step, 1)
                dve.wait_ge(vec_step, n(vec_step))
                stt(dst, dst, gain, r, MUL, MUL).then_inc(hs_normed, 1)
                dve.wait_ge(hs_normed, n(hs_normed))

            dve.wait_ge(hm_std, 1)
            V.reciprocal(rs[0:MANY, 0, :], rs[0:MANY, 0, :]).then_inc(hm_recip, 1)
            for t in range(MANY):
                dst = qkv[:, t, :] if t < 8 else (mix[:, t - 4, :] if t < 12 else kswn[:, t - 12, :])
                gain = SCALE if t < 4 else 1.0 if t < 8 else par("qnorm") if t < 12 else par("kn_slc" if t == 12 else "kn_win")
                dve.wait_ge(hm_bc, t + 1)
                stt(dst, dst, gain, PS[:, t % 4, :], MUL, MUL).then_inc(hm_normed, 1)
            dve.wait_ge(hm_normed, n(hm_normed) + MANY - 1)
            upper, strict = cst("upper"), cst("strict")
            for h in range(NH):
                tt(Ug[:, h], mid(upper, NC), last(gsm[:, 5, h::NH], P), MUL).then_inc(ug_ready if h == NH - 1 else vec_step, 1)
                dve.wait_ge(ug_ready if h == NH - 1 else vec_step, n(ug_ready if h == NH - 1 else vec_step))
            for h in range(NH):
                tt(Ib[:, h], mid(ident, NC), last(beta[:, :, h], P), MUL).then_inc(ug_ready if h == NH - 1 else vec_step, 1)
                dve.wait_ge(ug_ready if h == NH - 1 else vec_step, n(ug_ready if h == NH - 1 else vec_step))
            for h in range(NH):
                b = 4 * (h % 2)
                dve.wait_ge(prep_ps, h + 1)
                d, m = t1[:, h % 2, :], t2[:, h % 2, :]
                d3, m3 = (v.rearrange("p (c n) -> p c n", n=P) for v in (d, m))
                tt(d3, PS[:, b, :].rearrange("p (c n) -> p c n", n=P), last(gcl[:, 0, h::NH], P), SUB).then_inc(vec_step, 1)
                dve.wait_ge(vec_step, n(vec_step))
                ts(d, d, 0.0, None, MIN, ALU.bypass).then_inc(dec_in, 1)
                dve.wait_ge(dec_in, n(dec_in))
                tt(m3, PS[:, b + 1, :].rearrange("p (c n) -> p c n", n=P), mid(strict, NC), MUL).then_inc(vec_step, 1)
                dve.wait_ge(vec_step, n(vec_step))
                dve.wait_ge(eg_ready, h + 1)
                tt(qdT[:, h, :], qkv[:, h, :], eg, MUL).then_inc(vec_step, 1)
                dve.wait_ge(vec_step, n(vec_step))
                dve.wait_ge(dec_exp, h + 1)
                tt(d3, d3, mid(upper, NC), MUL).then_inc(vec_step, 1)
                dve.wait_ge(vec_step, n(vec_step))
                tt(flat(attnT[:, h]), PS[:, b + 3, :], d, MUL).then_inc(vec_step, 1)
                dve.wait_ge(vec_step, n(vec_step))
                tt(d, PS[:, b + 2, :], d, MUL).then_inc(vec_step, 1)
                dve.wait_ge(vec_step, n(vec_step))
                tt(flat(At[:, h]), d, m, MUL).then_inc(prep_done, 1)
                dve.wait_ge(prep_done, n(prep_done))
            for t in range(8):
                dve.wait_ge(tr_ready, t + 1)
                h = t % NH
                src = PS[:, t % 2, :].rearrange("p (c n) -> p c n", n=P)
                if t < NH:
                    tt(kd[:, h], src, last(e3[:, 0, h::NH], P), MUL).then_inc(vec_step, 1)
                    dve.wait_ge(vec_step, n(vec_step))
                    tt(kbg[:, h], src, last(kb[:, h::NH], P), MUL).then_inc(kv_done, 1)
                    dve.wait_ge(kv_done, n(kv_done))
                else:
                    tt(vb[:, h], src, last(beta[:, :, h], P), MUL).then_inc(kv_done, 1)
                    dve.wait_ge(kv_done, n(kv_done))

            def level(h, lv):
                b = CONST["levels"][0]
                mask = const[:, b:b + P] if isinstance(lv, int) and lv == 0 else const[:, bass.ds(lv * P + b, P)]
                tt(Am[:, h], At[:, h], mid(mask, NC), MUL).then_inc(am_ready, 1)
                dve.wait_ge(am_ready, n(am_ready))

            def update(h, i):
                dve.wait_ge(pq_done, i * NH + h + 1)
                tt(flat(Tm[:, h]), flat(Tm[:, h]), PS[:, 2 + h % 2, :], SUB).then_inc(vec_step, 1)
                dve.wait_ge(vec_step, n(vec_step))
                tt(flat(TT[:, h]), flat(TT[:, h]), PS[:, 4 + h % 2, :], SUB).then_inc(tt_ready, 1)
                dve.wait_ge(tt_ready, n(tt_ready))

            for h in range(NH):
                tt(Tm[:, h], mid(ident, NC), mid(ones, NC), MUL).then_inc(vec_step, 1)
                dve.wait_ge(vec_step, n(vec_step))
                tt(TT[:, h], mid(ident, NC), mid(ones, NC), MUL).then_inc(tt_ready, 1)
                dve.wait_ge(tt_ready, n(tt_ready))
                level(h, 0)
            with dve.Fori(0, LEVELS - 1) as i:
                n.enter(i, (tt_ready, NH), (am_ready, NH), (vec_step, NH))
                for h in range(NH):
                    update(h, i)
                    level(h, i + 1)
                n.leave(LEVELS - 1)
            for h in range(NH):
                update(h, LEVELS - 1)
            for h in range(NH):
                dve.wait_ge(uw_done, h + 1)
                copy(flat(wT[:, h]), PS[:, 2 * (h % 2) + 1, :]).then_inc(w_ready, 1)
                dve.wait_ge(w_ready, n(w_ready))
            for z in range(2):
                k_ = kcvc[:, z, :]
                win = bass.AP(k_.tensor, k_.offset, [list(k_.ap[0]), [1, CMP_L], [CMP_STRIDE, NCMP]])
                tt(kcp[:, z], win, last(par("pos_k" if z == 0 else "pos_v", 0, CMP_L), NCMP), ADD).then_inc(kcp_ready, 1)
                dve.wait_ge(kcp_ready, n(kcp_ready))
            V.memset(Sst, 0.0).then_inc(state_ready, 1)
            dve.wait_ge(state_ready, n(state_ready))
            for c in range(NC):
                dve.wait_ge(ws_done, c + 1)
                if c == 0:
                    dve.wait_ge(u_ready, NH)
                tt(vn, Um[:, :, c, :], PS[:, 0, :].rearrange("p (h n) -> p h n", n=P), SUB).then_inc(vnew_ready, 1)
                dve.wait_ge(vnew_ready, n(vnew_ready))
                dve.wait_ge(s_done, c + 1)
                for h in range(NH):
                    stt(Sst[:, h, :], Sst[:, h, :], e3[:, 2, c * NH + h:c * NH + h + 1], PS[:, 3, h * P:(h + 1) * P], MUL, ADD).then_inc(state_ready, 1)
                    dve.wait_ge(state_ready, n(state_ready))
            for h in range(NH):
                head_norm(h, oT[:, h, :], par("onorm"))
                tt(mix[:, h, :], mix[:, h, :], oT[:, h, :], MUL).then_inc(og_ready, 1)
                dve.wait_ge(og_ready, n(og_ready))
            dve.wait_ge(kc_ready, 1)
            head_norm(4, kct[:, :NCMP], par("kn_cmp"), NCMP)
            cneg = cst("cmpneg").rearrange("p (c n) -> p c n", n=NCMP)
            cmask = cst("cmpmask").rearrange("p (c n) -> p c n", n=NCMP)

            def prep(t):
                c, h = divmod(t, NH)
                N = (c + 1) * P
                m = mx[:, t % 2, :]
                dve.wait_ge(sc_done, t + 1)
                both = PS[:, 2 * (t % 2):2 * (t % 2) + 2, :N]
                tt(both[:, :, c * P:], both[:, :, c * P:], mid(cst("causal"), 2), ADD).then_inc(vec_step, 1)
                masked = n(vec_step)
                tt(sc[:, t % 2, :NCMP], PS[:, 4, :NCMP], cneg[:, c, :], ADD).then_inc(sc_ready, 1)
                dve.wait_ge(vec_step, masked)
                V.tensor_reduce(m[:, 1:3], both, X, MAX).then_inc(vec_step, 1)
                biggest = n(vec_step)
                dve.wait_ge(sc_ready, n(sc_ready))
                V.tensor_reduce(m[:, 0:1], sc[:, t % 2, :NCMP], X, MAX).then_inc(vec_step, 1)
                dve.wait_ge(vec_step, biggest)
                ts(m[:, 4:6], m[:, 1:3], -SCALE, None, MUL, ALU.bypass).then_inc(negm_ready, 1)
                dve.wait_ge(vec_step, n(vec_step))
                ts(sc[:, t % 2, :NCMP], sc[:, t % 2, :NCMP], m[:, 0:1], None, SUB, ALU.bypass).then_inc(sc_sub, 1)

            prep(0)
            for t in range(NC * NH):
                c, h = divmod(t, NH)
                N = (c + 1) * P
                m = mx[:, t % 2, :]
                if t + 1 < NC * NH:
                    prep(t + 1)
                dve.wait_ge(p_ready, 3 * (t + 1))
                V.reciprocal(m[:, 9:12], m[:, 6:9]).then_inc(vec_step, 1)
                dve.wait_ge(vec_step, n(vec_step))
                tt(m[:, 12:15], m[:, 9:12], sgm[:, c, NH + 3 * h:NH + 3 * h + 3], MUL).then_inc(vec_step, 1)
                dve.wait_ge(vec_step, n(vec_step))
                stt(Pc[:, t % 2, :NCMP], Pc[:, t % 2, :NCMP], m[:, 12:13], cmask[:, c, :], MUL, MUL).then_inc(pn_ready, 1)
                tt(Pm[:, t % 2, :, :N], Pm[:, t % 2, :, :N], last(m[:, 13:15], N), MUL).then_inc(pn_ready, 1)
                dve.wait_ge(pt_done, t + 1)
                if t >= 2:
                    dve.wait_ge(av_done, t - 1)
                copy(PT[:, t % 2, 4:5 + c, :], PS[:, 7, :N].rearrange("p (k q) -> p k q", q=P)).then_inc(pt_vec, 1)

            def residual(name, blk, col, ready, blocks=1):
                for m in range(KT):
                    dve.wait_ge(blocks_done, FIRST[name] + blocks * (m + 1))
                    stt(xT[:, m, :], PS[:, m % 4, :], mod[:, blk, col + m:col + m + 1], xT[:, m, :], MUL, ADD).then_inc(ready, 1)
                    dve.wait_ge(ready, n(ready))

            residual("w_out", 0, 16, x1_ready)
            norm(1)
            with dve.Fori(0, FT // 2) as i:
                n.enter(i, (fy_ready, 4), (ff_ready, 2), (vec_step, 8 + SLOTS), (ada_2_used, SLOTS))
                matvec(1, i, ring_2, slot_2_ready, ada_2_used, acc_2[:, bass.ds(i, 1), :].rearrange("p o n -> p (o n)"))
                for u in range(2):
                    for z in range(2):
                        j = 2 * u + z
                        dve.wait_ge(blocks_done, FIRST["up"] + i * 4 + j + 1)

                        def tap(s_):
                            return param[:, bass.ds(i * 12 + (PARAM["fconv"][0] + 3 * j + s_), 1)]
                        o = (y0 if z == 0 else y1)[:, u, :]
                        ts(o, PS[:, j, :], tap(2), param[:, bass.ds(i * 4 + (PARAM["fbias"][0] + j), 1)], MUL, ADD).then_inc(vec_step, 1)
                        dve.wait_ge(vec_step, n(vec_step))
                        for s_ in (1, 2):
                            stt(o[:, s_:], PS[:, j, :S - s_], tap(2 - s_), o[:, s_:], MUL, ADD).then_inc(fy_ready if s_ == 2 else vec_step, 1)
                            dve.wait_ge(fy_ready if s_ == 2 else vec_step, n(fy_ready if s_ == 2 else vec_step))
                    dve.wait_ge(sa_ready, i * 2 + u + 1)
                    tt(gT[:, bass.ds(i * 2 + u, 1), :].rearrange("p o n -> p (o n)"), sa[:, u, :], y1[:, u, :], MUL).then_inc(ff_ready, 1)
                    dve.wait_ge(ff_ready, n(ff_ready))
                n.leave(FT // 2)
            matvec(1, FT // 2, ring_2, slot_2_ready, ada_2_used, acc_2[:, FT // 2, :])
            residual("down", 0, 40, x2_ready, 2)
            modulation(1)
            norm(2)
            V.memset(pT[:, :, :16], 0.0).then_inc(vec_step, 1)
            dve.wait_ge(vec_step, n(vec_step))
            V.memset(glu[:, :, :30], 0.0).then_inc(vec_step, 1)
            dve.wait_ge(vec_step, n(vec_step))
            V.memset(cs1[:, :16], 0.0).then_inc(vec_step, 1)
            dve.wait_ge(vec_step, n(vec_step))
            V.memset(cs2[:, :16], 0.0).then_inc(vec_step, 1)
            dve.wait_ge(vec_step, n(vec_step))
            cnt = cst("poolcnt").rearrange("p (g n) -> p g n", n=16)
            for g in range(4):
                dve.wait_ge(sg_ready, g + 1)
                src = pT[:, g, :]
                for s_ in range(g + 1):
                    dst = (cs1, cs2)[s_ % 2]
                    d_ = 1 << s_
                    tt(dst[:, 16:], src[:, 16:], src[:, 16 - d_:16 + S - d_], ADD).then_inc(vec_step, 1)
                    dve.wait_ge(vec_step, n(vec_step))
                    src = dst
                w = PW[g]
                tt(src[:, 16:16 + w], src[:, 16:16 + w], cnt[:, g, :w], MUL).then_inc(vec_step, 1)
                dve.wait_ge(vec_step, n(vec_step))
                stt(mx4[:, g, :w], pT[:, g, 16:16 + w], -1.0, src[:, 16:16 + w], MUL, ADD).then_inc(vec_step, 1)
                dve.wait_ge(vec_step, n(vec_step))
                stt(mx4[:, g, w:], src[:, 16 + w:], 1.0 / w, pT[:, g, 16 + w:], MUL, SUB).then_inc(pm_ready, 1)
                dve.wait_ge(pm_ready, n(pm_ready))
            for t in range(4):
                dve.wait_ge(sg_ready, 4 + 2 * t + 2)
                tt(glu[:, t, 30:], a1[:, t % 2, :], a2[:, t % 2, :], MUL).then_inc(glu_ready, 1)
                dve.wait_ge(glu_ready, n(glu_ready))
            for t in range(4):
                ts(yc[:, t, :], glu[:, t, 30:], par("dw", t * TAPS + TAPS - 1), par("dwb", t), MUL, ADD).then_inc(vec_step, 1)
                dve.wait_ge(vec_step, n(vec_step))
            for s_ in range(1, TAPS):
                for t in range(4):
                    stt(yc[:, t, :], glu[:, t, 30 - s_:30 - s_ + S], par("dw", t * TAPS + TAPS - 1 - s_), yc[:, t, :], MUL, ADD).then_inc(ln_in if s_ == TAPS - 1 and t == 3 else vec_step, 1)
                    dve.wait_ge(ln_in if s_ == TAPS - 1 and t == 3 else vec_step, n(ln_in if s_ == TAPS - 1 and t == 3 else vec_step))
            dve.wait_ge(ln_mu, 1)
            for g in range(4):
                tt(yc[:, g, :], yc[:, g, :], lnm, SUB).then_inc(ln_y, 1)
                dve.wait_ge(ln_y, n(ln_y))
            dve.wait_ge(ln_std, 1)
            V.reciprocal(rs[:, 0, :], rs[:, 0, :]).then_inc(vec_step, 1)
            dve.wait_ge(vec_step, n(vec_step))
            for g in range(4):
                tt(yc[:, g, :], yc[:, g, :], rs[:, 0, :], MUL).then_inc(vec_step, 1)
                dve.wait_ge(vec_step, n(vec_step))
                ts(yc[:, g, :], yc[:, g, :], par("lng", g), par("lnb", g), MUL, ADD).then_inc(ln_y, 1)
                dve.wait_ge(ln_y, n(ln_y))
            for m in range(KT):
                dve.wait_ge(blocks_done, FIRST["branch"] + m + 1)
                b = 2 * (m % 2)
                tt(m1[:, 0, :], PS[:, b, :], sgT[:, m, :], MUL).then_inc(vec_step, 1)
                dve.wait_ge(vec_step, n(vec_step))
                tt(m1[:, 1, :], PS[:, b + 1, :], sgT[:, 8 + m, :], MUL).then_inc(m_half, 1)
                dve.wait_ge(m_half, n(m_half))
                tt(mg[:, m, :], m1[:, 0, :], m1[:, 1, :], ADD).then_inc(merged, 1)
                dve.wait_ge(merged, n(merged))
            residual("w_out_2", 1, 16, x3_ready)
            norm(3)
            iota = cst("iota")

            def top16(src, val, ind, scratch):
                dve.sem_inc(vec_seen, 1)
                V.max(val[:, 0:8], src).then_inc(vec_step, 1)
                dve.wait_ge(vec_step, n(vec_step))
                dve.sem_inc(vec_seen, 1)
                V.max_index(ind[:, 0:8], val[:, 0:8], src).then_inc(vec_step, 1)
                dve.wait_ge(vec_step, n(vec_step))
                dve.sem_inc(vec_seen, 1)
                V.match_replace(scratch, val[:, 0:8], src, NEG).then_inc(vec_step, 1)
                dve.wait_ge(vec_step, n(vec_step))
                dve.sem_inc(vec_seen, 1)
                V.max(val[:, 8:16], scratch).then_inc(vec_step, 1)
                dve.wait_ge(vec_step, n(vec_step))
                dve.sem_inc(vec_seen, 1)
                V.max_index(ind[:, 8:16], val[:, 8:16], scratch).then_inc(vec_step, 1)
                dve.wait_ge(vec_step, n(vec_step))

            def route_keys(s_):
                copy(scur.rearrange("p z n -> p (z n)"), sS[:, bass.ds(s_, 1), :].rearrange("p o n -> p (o n)")).then_inc(vec_step, 1)
                dve.wait_ge(vec_step, n(vec_step))
                for z in range(2):
                    top16(scur[:, z, :], vcur[:, z, :], icur[:, z, :], s2[:, :NKEYS])

            def route_experts(s_, u, fresh=False):
                copy(idf, icur[:]).then_inc(vec_step, 1)
                dve.wait_ge(vec_step, n(vec_step))
                tt(cand.rearrange("p (x y) -> p x y", y=16), last(vcur[:, 0, :], 16), mid(vcur[:, 1, :], 16), ADD).then_inc(vec_step, 1)
                dve.wait_ge(vec_step, n(vec_step))
                top16(cand, tcur, pcur[:], s2)
                V.tensor_scalar(pab[:, 0, :], pcur[:], 4, None, ALU.logical_shift_right).then_inc(vec_step, 1)
                dve.wait_ge(vec_step, n(vec_step))
                V.tensor_scalar(pab[:, 1, :], pcur[:], 15, None, ALU.bitwise_and).then_inc(vec_step, 1)
                dve.wait_ge(vec_step, n(vec_step))
                copy(ifl, pab[:]).then_inc(vec_step, 1)
                dve.wait_ge(vec_step, n(vec_step))
                tt(eqv, last(ifl, 16), mid(iota, 2, 16), ALU.is_equal).then_inc(vec_step, 1)
                dve.wait_ge(vec_step, n(vec_step))
                tt(eqv, eqv, idf.unsqueeze(2).to_broadcast([P, 2, 16, 16]), MUL).then_inc(vec_step, 1)
                dve.wait_ge(vec_step, n(vec_step))
                V.tensor_reduce(sel.rearrange("p z k -> p (z k)"), eqv.rearrange("p z k x -> p (z k) x"), X, ADD).then_inc(vec_step, 1)
                dve.wait_ge(vec_step, n(vec_step))
                stt(exf, sel[:, 0, :], float(NKEYS), sel[:, 1, :], MUL, ADD).then_inc(vec_step, 1)
                dve.wait_ge(vec_step, n(vec_step))
                copy(ecur[:, u, :], exf).then_inc(ecur_ready, 1)
                dve.wait_ge(ecur_ready, n(ecur_ready))
                if not fresh:
                    dve.wait_ge(w_ready2, s_ * TOPK - TOPK)
                tt(gcur[:, u, :], tcur, tcur[:, 0:1].to_broadcast([P, 16]), SUB).then_inc(sm_in, 1)
                dve.wait_ge(sm_in, n(sm_in))
                dve.wait_ge(sm_exp, s_ + 1)
                V.reciprocal(gsum[:, u, 1:2], gsum[:, u, 0:1]).then_inc(vec_step, 1)
                dve.wait_ge(vec_step, n(vec_step))
                ts(gcur[:, u, :], gcur[:, u, :], gsum[:, u, 1:2], None, MUL, ALU.bypass).then_inc(gate_ready, 1)
                dve.wait_ge(gate_ready, n(gate_ready))

            def rows_dot(s_, c, first_pair, more):
                for j in range(TOPK):
                    if j == 8 and more:
                        route_keys(s_ + 2)
                    if first_pair and j == 4 and c:
                        add_tile(c - 1)
                    if first_pair and j == 12 and c > 1:
                        last_norm(c - 2)
                    r = j % RING
                    dve.wait_ge(row_landed[r], s_ * 32 + 16 * (j // RING + 1))
                    V.tensor_tensor_reduce(out=junk, in0=ring_e[:, r, :D], in1=hrow[:, c, :], scale=1.0, scalar=0.0,
                                           op0=MUL, op1=ADD, accum_out=dots[:, (j // BATCH) % NB, j % BATCH:j % BATCH + 1]
                                           ).then_inc(dots_ready, 1)
                    dve.wait_ge(dots_ready, n(dots_ready))

            def pair(i, c, more, first_pair=False):
                for u in range(2):
                    rows_dot(i * 2 + (c * HEADS + u), c, first_pair and u == 1, more)
                    if more:
                        route_experts(i * 2 + (c * HEADS + u + 2), u)

            def add_tile(c):
                for v in range(2):
                    dve.wait_ge(pt2_done, 2 * c + v + 1)
                    for k in range(4):
                        m = 4 * v + k
                        o = xT[:, m, c * P:(c + 1) * P]
                        stt(o, PS[:, 2 + v, k * P:(k + 1) * P], mod[:, 1, 40 + m:41 + m], o, MUL, ADD).then_inc(x4_ready, 1)
                        dve.wait_ge(x4_ready, n(x4_ready))

            def last_norm(c):
                o = xT[:, :, c * P:(c + 1) * P]
                r = rs[:, c % 2, 0:P]
                dve.wait_ge(fin_std, c + 1)
                V.reciprocal(r, r).then_inc(vec_step, 1)
                dve.wait_ge(vec_step, n(vec_step))
                tt(o, o, mid(r, KT), MUL).then_inc(vec_step, 1)
                dve.wait_ge(vec_step, n(vec_step))
                tt(o, o, last(par("final", 0, KT), P), MUL).then_inc(fin_ready, 1)

            dve.wait_ge(sc2_ready, 1)
            for u in range(2):
                route_keys(u)
                route_experts(u, u, True)
            for t in range(2 * NC):
                c, half = divmod(t, 2)
                dve.wait_ge(hr_done, t + 1)
                copy(hrow[:, c, half * S:(half + 1) * S], PS[:, 4 + t % 2, :]).then_inc(hr_ready, 1)
                dve.wait_ge(hr_ready, n(hr_ready))
            dve.wait_ge(sc2_ready, 4 * NC)
            for c in range(NC):
                pair(0, c, True, first_pair=True)
                end = c == NC - 1
                with dve.Fori(1, 3 if end else 4) as i:
                    n.enter(i - 1, (dots_ready, 2 * TOPK), (vec_step, 2 * 26), (ecur_ready, 2), (sm_in, 2), (gate_ready, 2))
                    pair(i, c, True)
                    n.leave(2 if end else 3)
                if end:
                    pair(3, c, False)
            add_tile(NC - 1)
            last_norm(NC - 2)
            last_norm(NC - 1)

        @block.gpsimd
        def _(pool):
            pool.wait_ge(att_ready, NC * NH)
            for j in range(SLOTS):
                pool.dma_start(ring_2[:, j, :], a["ada_2"][j]).then_inc(slot_2_ready[j], 16)
            with pool.Fori(1, 12) as i:
                for j in range(SLOTS):
                    pool.wait_ge(ada_2_used, i * SLOTS + j - SLOTS + 1)
                    pool.dma_start(ring_2[:, j, :],
                                   a["ada_2"][bass.ds(i * SLOTS + j, 1)].rearrange("o p n -> p (o n)")
                                   ).then_inc(slot_2_ready[j], 16)

            def rows(s_, u, first=False):
                pool.wait_ge(ecur_ready, s_ + 1)
                pool.sem_inc(pool_seen, 1)
                for j in range(TOPK):
                    if first and j == RING // 2:
                        pool.wait_ge(sc2_ready, 4 * NC)
                        pool.sem_inc(pool_seen, 1)
                    if j % BATCH == 0 and not (first and j < RING):
                        pool.wait_ge(rows_used, s_ * SB + (j // BATCH - NB + 1))
                        pool.sem_inc(pool_seen, 1)
                    nc.gpsimd.indirect_dma_start(
                        out=ring_e[:, j % RING, :], out_offset=None, in_=a["experts"],
                        in_offset=bass.IndirectOffsetOnAxis(ap=ecur[:, u, j:j + 1], axis=0)
                    ).then_inc(row_landed[j % RING], 16)

            rows(0, 0, True)
            with pool.Fori(0, STEPS // 2 - 1) as i:
                rows(i * 2 + 1, 1)
                rows(i * 2 + 2, 0)
            rows(STEPS - 1, 1)


def tiles_of(w):
    k, n = w.shape
    return np.ascontiguousarray(w.reshape(k // P, P, n // P, P).transpose(2, 1, 0, 3).reshape(n // P, P, k))


def rows_of(w):
    k, n = w.shape
    return np.ascontiguousarray(w.reshape(4, 2, P, n // S, S).transpose(3, 0, 2, 1, 4).reshape(-1, P, 2 * S))


def cols(v):
    return np.asarray(v).reshape(-1, P).T


def constants():
    c = np.zeros((P, NCONST), np.float32)
    i = np.arange(P)

    def put(name, v):
        c[:, CONST[name][0]:CONST[name][1]] = np.asarray(v).reshape(P, -1)

    put("ident", np.eye(P))
    put("ones", np.ones((P, P)))
    put("upper", i[:, None] <= i[None, :])
    put("strict", i[:, None] < i[None, :])
    put("causal", np.where(i[None, :] <= i[:, None], 0.0, NEG))
    lv = []
    for l in range(LEVELS):
        b = 1 << l
        same = i[:, None] // (2 * b) == i[None, :] // (2 * b)
        lv.append(same & ((i[:, None] // b) % 2 == 0) & ((i[None, :] // b) % 2 == 1))
    put("levels", np.stack(lv, 1))
    t = np.arange(NC)[None, :, None] * P + i[:, None, None]
    seen = np.arange(NCMP)[None, None, :] * CMP_STRIDE + CMP_L - 1 <= t
    put("cmpneg", np.where(seen, 0.0, NEG))
    put("cmpmask", seen)
    cnt = np.stack([1.0 / np.minimum(np.arange(1, 17), w) for w in PW])
    put("poolcnt", np.broadcast_to(cnt[None], (P, 4, 16)))
    put("iota", np.broadcast_to(np.arange(16.0), (P, 16)))
    strip = np.zeros((P, 2 * MANY - 1))
    strip[:, MANY - 1] = 1.0
    put("strip", strip)
    put("hscale", np.where(i < 8, 1.0, 1.0 / HD))
    put("eps", np.full((P, 1), EPS))
    put("one", np.ones((P, 1)))
    return c


def layout(i):
    g = {k: np.asarray(v) for k, v in i.items()}
    a = {"const": constants()}
    a["select"] = np.ascontiguousarray(np.broadcast_to(np.eye(MANY, dtype=np.float32)[:, :, None], (MANY, MANY, P)))
    a["x"] = np.ascontiguousarray(g["x"][0].T.reshape(KT, P, S).transpose(1, 0, 2))
    w = g["w_in"][0]
    W4 = NH * HD
    at = np.cumsum([0, W4, W4, W4, W4, NH, NH, W4] + [HD] * 6 + [3 * NH])
    part = [w[:, at[n]:at[n + 1]] for n in range(14)]
    a["w_in"] = tiles_of(np.concatenate([part[n] for n in (0, 1, 2, 3, 6, 7, 8, 9, 11)], 1))
    rw = np.concatenate([part[n] for n in (10, 12, 4, 5, 13)], 1)
    a["roww"] = np.ascontiguousarray(rw.reshape(KT, P, NROW).transpose(1, 0, 2))
    a["ada"], a["ada_2"] = rows_of(g["ada_w"][0]), rows_of(g["ada_w_2"][0])
    a["cmp"] = np.ascontiguousarray(np.stack([g["cmp_k_w1"][0], g["cmp_v_w1"][0]])
                                    .reshape(8, KT, P, P).transpose(0, 2, 1, 3).reshape(8, P, D))
    a["w_out"], a["w_out_2"], a["query"] = tiles_of(g["w_out"][0]), tiles_of(g["w_out_2"][0]), tiles_of(g["w_query_2"][0])
    up = tiles_of(g["ffn_w_up"][0])
    pair = np.arange(2 * FT).reshape(2, FT).T.ravel()
    a["up"] = np.ascontiguousarray(up[pair])
    a["down"] = np.ascontiguousarray(tiles_of(g["ffn_w_down"][0]).reshape(KT, P, 2, WIDE).transpose(0, 2, 1, 3).reshape(16, P, WIDE))
    order = np.array([0, 1, 2, 3, 4, 8, 5, 9, 6, 10, 7, 11] + list(range(12, 28)))
    a["w_in_2"] = np.ascontiguousarray(tiles_of(g["w_in_2"][0])[order])
    a["branch"] = np.ascontiguousarray(np.concatenate([tiles_of(g["pool_up_2"][0]), tiles_of(g["conv_out_2"][0])], 2))
    a["experts"] = np.concatenate([g["expert_u_2"][0], g["expert_v_2"][0]], 1)
    m = np.zeros((P, NMATS), np.float32)
    for n, v in (("w2k", g["cmp_k_w2"][0]), ("w2v", g["cmp_v_w2"][0]), ("keys1", g["sub_keys_1_2"][0].T),
                 ("keys2", g["sub_keys_2_2"][0].T), ("poolw", g["pool_w_2"][0].transpose(1, 0, 2).reshape(P, -1))):
        m[:, MATS[n][0]:MATS[n][1]] = v
    a["mats"] = m
    p = np.zeros((P, NPARAM), np.float32)

    def put(name, v):
        p[:, PARAM[name][0]:PARAM[name][1]] = v

    put("c", cols(g["c"][0])); put("c_2", cols(g["c_2"][0]))
    put("ada_b", cols(g["ada_b"][0])); put("ada_b_2", cols(g["ada_b_2"][0]))
    put("norm1", cols(g["norm1_w"][0])); put("norm2", cols(g["norm2_w"][0]))
    put("norm1_2", cols(g["norm1_g_2"][0])); put("norm2_2", cols(g["norm2_g_2"][0])); put("final", cols(g["final_g_2"]))
    put("gconv", g["gdn_conv_w"][0].reshape(4, 12, P).transpose(2, 1, 0).reshape(P, -1))
    put("a_log", np.broadcast_to(np.tile(g["gdn_A_log"][0], NC), (P, 16)))
    put("dt", np.broadcast_to(np.tile(g["gdn_dt_bias"][0], NC), (P, 16)))
    for n, k in (("onorm", "gdn_out_norm_w"), ("qnorm", "nsa_q_norm_w"), ("kn_cmp", "nsa_k_norm_cmp"),
                 ("kn_slc", "nsa_k_norm_slc"), ("kn_win", "nsa_k_norm_win")):
        put(n, cols(g[k][0]))
    put("pos_k", g["cmp_k_pos"][0].T); put("pos_v", g["cmp_v_pos"][0].T)
    put("fconv", g["ffn_conv_w"][0].reshape(3, 2 * FT, P)[:, pair].transpose(2, 1, 0).reshape(P, -1))
    put("fbias", cols(g["ffn_conv_b"][0])[:, pair])
    put("b_in", cols(g["b_in_2"][0])[:, order])
    put("pscale", cols(g["pool_scale_2"][0]))
    put("dw", g["dw_kernel_2"][0].reshape(TAPS, 4, P).transpose(2, 1, 0).reshape(P, -1))
    put("dwb", cols(g["dw_bias_2"][0])); put("lng", cols(g["conv_ln_g_2"][0])); put("lnb", cols(g["conv_ln_b_2"][0]))
    a["param"] = p
    return a


def program(nc, arrays):
    aps = {n: nc.dram_tensor(f"{n}_dram", v.shape, F32, kind="ExternalInput").ap() for n, v in arrays.items()}
    out = nc.dram_tensor("out_dram", (P, KT, S), F32, kind="ExternalOutput").ap()
    build(nc, aps, out)


def kernel(**inputs):
    from concourse.bass_utils import run_bass_kernel_spmd
    import concourse.bacc as bacc
    arrays = layout(inputs)
    nc = bacc.Bacc("TRN2", target_bir_lowering=False, num_devices=1)
    program(nc, arrays)
    r = run_bass_kernel_spmd(nc, [{f"{n}_dram": v for n, v in arrays.items()}], core_ids=[0])
    got = r.results[0]["out_dram"]
    return np.ascontiguousarray(got.transpose(2, 1, 0).reshape(1, S, D))
```
